# Optimizing a Trainium2 kernel written in Bass

```python
import jax, jax.numpy as jnp
from jax import lax
import numpy as np

D_MODEL = 2048
BATCH = 1
SEQ = 256
DEPTH = 1

FOX_HEADS = 8
FOX_HD = 128
FOX_WIDTH = FOX_HEADS * FOX_HD
Q_BLOCK = 128
MLSTM_HEADS = 4
MLSTM_DQK = 128
MLSTM_DV = 256
MLSTM_QK_WIDTH = MLSTM_HEADS * MLSTM_DQK
MLSTM_V_WIDTH = MLSTM_HEADS * MLSTM_DV
MLSTM_CHUNK = 64
D_FF = 5632
CONV_W = 3
EPS = 1e-6

OFF_FQ = 0
OFF_FK = OFF_FQ + FOX_WIDTH
OFF_FV = OFF_FK + FOX_WIDTH
OFF_FF = OFF_FV + FOX_WIDTH
OFF_MQ = OFF_FF + FOX_HEADS
OFF_MK = OFF_MQ + MLSTM_QK_WIDTH
OFF_MV = OFF_MK + MLSTM_QK_WIDTH
OFF_MO = OFF_MV + MLSTM_V_WIDTH
OFF_MI = OFF_MO + MLSTM_V_WIDTH
OFF_MF = OFF_MI + MLSTM_HEADS
OFF_GA = OFF_MF + MLSTM_HEADS
OFF_GM = OFF_GA + D_MODEL
D_IN = OFF_GM + D_MODEL


def rmsnorm(x, g):
    x32 = x.astype(jnp.float32)
    y = x32 * lax.rsqrt(jnp.mean(x32 * x32, axis=-1, keepdims=True) + EPS)
    return (y * g.astype(jnp.float32)).astype(x.dtype)

def forgetting_attention(q, k, v, log_f):
    B, S, H, D = q.shape
    F = jnp.cumsum(log_f, axis=1).transpose(0, 2, 1)
    scale = D ** -0.5
    outs = []
    for blk in range(S // Q_BLOCK):
        q0, q1 = blk * Q_BLOCK, (blk + 1) * Q_BLOCK
        qb = q[:, q0:q1].astype(jnp.float32)
        kb = k[:, :q1].astype(jnp.float32)
        vb = v[:, :q1]
        logits = jnp.einsum('bqhd,bkhd->bhqk', qb, kb) * scale
        logits = logits + F[:, :, q0:q1, None] - F[:, :, None, :q1]
        q_pos = q0 + jnp.arange(Q_BLOCK)
        k_pos = jnp.arange(q1)
        causal = k_pos[None, :] <= q_pos[:, None]
        logits = jnp.where(causal, logits, -jnp.inf)
        p = jax.nn.softmax(logits, axis=-1)
        outs.append(jnp.einsum('bhqk,bkhd->bqhd', p.astype(vb.dtype), vb))
    return jnp.concatenate(outs, axis=1)

def mlstm_chunkwise(q, k, v, i_pre, log_f):
    B, S, H, DK = q.shape
    DV = v.shape[-1]
    L = MLSTM_CHUNK
    NC = S // L
    f32 = jnp.float32

    def chunks(a):
        return a.astype(f32).reshape(B, NC, L, H, a.shape[-1]).transpose(1, 0, 3, 2, 4)

    def gchunks(a):
        return a.astype(f32).reshape(B, NC, L, H).transpose(1, 0, 3, 2)

    qc = chunks(q) * (DK ** -0.5)
    kc, vc = chunks(k), chunks(v)
    ic, fc = gchunks(i_pre), gchunks(log_f)
    causal = jnp.tril(jnp.ones((L, L), dtype=bool))

    def step(carry, inp):
        C, n, m = carry
        qt, kt, vt, it, ft = inp
        b = jnp.cumsum(ft, axis=-1)
        dlog = b[..., :, None] - b[..., None, :] + it[..., None, :]
        dlog = jnp.where(causal, dlog, -jnp.inf)
        inter = b + m[..., None]
        m_row = jnp.maximum(inter, dlog.max(axis=-1))
        s = jnp.einsum('bhtd,bhsd->bhts', qt, kt) * jnp.exp(dlog - m_row[..., None])
        inter_w = jnp.exp(inter - m_row)
        num = inter_w[..., None] * jnp.einsum('bhtd,bhde->bhte', qt, C) + jnp.einsum('bhts,bhse->bhte', s, vt)
        den = inter_w * jnp.einsum('bhtd,bhd->bht', qt, n) + s.sum(axis=-1)
        h = num / jnp.maximum(jnp.abs(den), jnp.exp(-m_row))[..., None]
        bL = b[..., -1]
        w_log = bL[..., None] - b + it
        m_new = jnp.maximum(bL + m, w_log.max(axis=-1))
        decay = jnp.exp(bL + m - m_new)
        ws = jnp.exp(w_log - m_new[..., None])
        C_new = decay[..., None, None] * C + jnp.einsum('bhs,bhsd,bhse->bhde', ws, kt, vt)
        n_new = decay[..., None] * n + jnp.einsum('bhs,bhsd->bhd', ws, kt)
        return (C_new, n_new, m_new), h

    init = (jnp.zeros((B, H, DK, DV), f32), jnp.zeros((B, H, DK), f32), jnp.zeros((B, H), f32))
    _, hs = lax.scan(step, init, (qc, kc, vc, ic, fc))
    return hs.transpose(1, 0, 3, 2, 4).reshape(B, S, H, DV).astype(v.dtype)

def causal_dwconv(u, w, b):
    S = u.shape[1]
    up = jnp.pad(u, ((0, 0), (CONV_W - 1, 0), (0, 0)))
    out = b
    for j in range(CONV_W):
        out = out + up[:, j:j + S] * w[j]
    return out

def first_inputs(seed: int = 0) -> dict:
    key = jax.random.key(seed)
    ks = jax.random.split(key, 20)
    nrm = lambda k, shape, s: jax.random.normal(k, shape, jnp.float32) * s
    L = DEPTH
    return {
        "x": nrm(ks[0], (BATCH, SEQ, D_MODEL), 1.0),
        "norm1_g": 1.0 + nrm(ks[1], (L, D_MODEL), 0.1),
        "w_in": nrm(ks[2], (L, D_MODEL, D_IN), D_MODEL ** -0.5),
        "fox_f_bias": jnp.linspace(1.0, 4.0, FOX_HEADS, dtype=jnp.float32)[None] + nrm(ks[3], (L, FOX_HEADS), 0.1),
        "q_norm_g": 1.0 + nrm(ks[4], (L, FOX_HD), 0.1),
        "k_norm_g": 1.0 + nrm(ks[5], (L, FOX_HD), 0.1),
        "m_i_bias": nrm(ks[6], (L, MLSTM_HEADS), 0.1),
        "m_f_bias": jnp.linspace(3.0, 6.0, MLSTM_HEADS, dtype=jnp.float32)[None] + nrm(ks[7], (L, MLSTM_HEADS), 0.1),
        "m_norm_g": 1.0 + nrm(ks[8], (L, MLSTM_HEADS, MLSTM_DV), 0.1),
        "w_proj_a": nrm(ks[9], (L, FOX_WIDTH, D_MODEL), FOX_WIDTH ** -0.5),
        "w_proj_m": nrm(ks[10], (L, MLSTM_V_WIDTH, D_MODEL), MLSTM_V_WIDTH ** -0.5),
        "w_out": nrm(ks[11], (L, D_MODEL, D_MODEL), D_MODEL ** -0.5),
        "norm2_g": 1.0 + nrm(ks[12], (L, D_MODEL), 0.1),
        "w_up": nrm(ks[13], (L, D_MODEL, 2 * D_FF), D_MODEL ** -0.5),
        "conv_w": nrm(ks[14], (L, CONV_W, 2 * D_FF), CONV_W ** -0.5),
        "conv_b": nrm(ks[15], (L, 2 * D_FF), 0.02),
        "w_down": nrm(ks[16], (L, D_FF, D_MODEL), D_FF ** -0.5),
    }

def first_block(x, norm1_g, w_in, fox_f_bias, q_norm_g, k_norm_g, m_i_bias, m_f_bias,
              m_norm_g, w_proj_a, w_proj_m, w_out, norm2_g, w_up, conv_w, conv_b, w_down):
    B, S, _ = x.shape

    for l in range(DEPTH):
        h = rmsnorm(x, norm1_g[l])
        z = jnp.einsum('bsd,de->bse', h, w_in[l])

        fq = rmsnorm(z[..., OFF_FQ:OFF_FK].reshape(B, S, FOX_HEADS, FOX_HD), q_norm_g[l])
        fk = rmsnorm(z[..., OFF_FK:OFF_FV].reshape(B, S, FOX_HEADS, FOX_HD), k_norm_g[l])
        fv = z[..., OFF_FV:OFF_FF].reshape(B, S, FOX_HEADS, FOX_HD)
        f_logf = jax.nn.log_sigmoid((z[..., OFF_FF:OFF_MQ] + fox_f_bias[l]).astype(jnp.float32))
        a_out = forgetting_attention(fq, fk, fv, f_logf).reshape(B, S, FOX_WIDTH)

        mq = z[..., OFF_MQ:OFF_MK].reshape(B, S, MLSTM_HEADS, MLSTM_DQK)
        mk = z[..., OFF_MK:OFF_MV].reshape(B, S, MLSTM_HEADS, MLSTM_DQK)
        mv = z[..., OFF_MV:OFF_MO].reshape(B, S, MLSTM_HEADS, MLSTM_DV)
        m_o = jax.nn.sigmoid(z[..., OFF_MO:OFF_MI]).reshape(B, S, MLSTM_HEADS, MLSTM_DV)
        m_ipre = (z[..., OFF_MI:OFF_MF] + m_i_bias[l]).astype(jnp.float32)
        m_logf = jax.nn.log_sigmoid((z[..., OFF_MF:OFF_GA] + m_f_bias[l]).astype(jnp.float32))
        hm = mlstm_chunkwise(mq, mk, mv, m_ipre, m_logf)
        m_out = (rmsnorm(hm, m_norm_g[l]) * m_o).reshape(B, S, MLSTM_V_WIDTH)

        g_a = jax.nn.sigmoid(z[..., OFF_GA:OFF_GM])
        g_m = jax.nn.sigmoid(z[..., OFF_GM:D_IN])
        merged = (g_a * jnp.einsum('bse,ed->bsd', a_out, w_proj_a[l])
                  + g_m * jnp.einsum('bse,ed->bsd', m_out, w_proj_m[l]))
        x = x + jnp.einsum('bsd,de->bse', merged, w_out[l])

        h2 = rmsnorm(x, norm2_g[l])
        u = causal_dwconv(jnp.einsum('bsd,df->bsf', h2, w_up[l]), conv_w[l], conv_b[l])
        u_gate, u_val = u[..., :D_FF], u[..., D_FF:]
        x = x + jnp.einsum('bsf,fd->bsd', jax.nn.silu(u_gate) * u_val, w_down[l])
    return x


D_MIX = D_MODEL
GM_WIDTH = D_MIX // 2
LRU_WIDTH = D_MIX - GM_WIDTH
CHUNK = 128
GM_HEADS = 8
GM_HEAD_DIM = GM_WIDTH // GM_HEADS
LRU_HEADS = 8
LRU_BLOCK = LRU_WIDTH // LRU_HEADS
LRU_CONV = 4
LRU_C = 8.0
FFN_MULT = 3
D_FF_2 = FFN_MULT * D_MODEL
FFN_CONV = 3
IN_COLS = 2 * GM_WIDTH + 2 * LRU_WIDTH
RMS_EPS = 1e-6
LN_EPS = 1e-5


def _rmsnorm(x, g):
    xf = x.astype(jnp.float32)
    y = xf * lax.rsqrt(jnp.mean(xf * xf, axis=-1, keepdims=True) + RMS_EPS)
    return (y * g.astype(jnp.float32)).astype(x.dtype)

def _layernorm(x, g, b):
    xf = x.astype(jnp.float32)
    mu = jnp.mean(xf, axis=-1, keepdims=True)
    xc = xf - mu
    y = xc * lax.rsqrt(jnp.mean(xc * xc, axis=-1, keepdims=True) + LN_EPS)
    return (y * g.astype(jnp.float32) + b.astype(jnp.float32)).astype(x.dtype)

def _causal_dwconv(x, w, b):
    k_width = w.shape[0]
    s = x.shape[1]
    xp = jnp.pad(x, ((0, 0), (k_width - 1, 0), (0, 0)))
    y = b
    for k in range(k_width):
        y = y + xp[:, k:k + s] * w[k]
    return y

def _spatial_gating(z, v_g, v_b, ws, bs):
    u, v = jnp.split(z, 2, axis=-1)
    v = _layernorm(v, v_g, v_b)
    bsz, s, _ = v.shape
    vc = v.reshape(bsz, s // CHUNK, CHUNK, GM_HEADS, GM_HEAD_DIM)
    mask = jnp.tril(jnp.ones((CHUNK, CHUNK), dtype=bool))
    w = jnp.where(mask[None], ws, jnp.zeros((), ws.dtype))
    mixed = jnp.einsum('hts,bcshd->bcthd', w, vc) + bs.T[None, None, :, :, None]
    return u * mixed.reshape(bsz, s, GM_WIDTH)

def _lru_combine(left, right):
    a1, b1 = left
    a2, b2 = right
    return a1 * a2, a2 * b1 + b2

def _rg_lru(x, wa, ba, wx, bx, lam):
    bsz, s, w = x.shape
    xh = x.reshape(bsz, s, LRU_HEADS, LRU_BLOCK)
    r = jax.nn.sigmoid(jnp.einsum('bshi,hij->bshj', xh, wa) + ba).reshape(bsz, s, w)
    i = jax.nn.sigmoid(jnp.einsum('bshi,hij->bshj', xh, wx) + bx).reshape(bsz, s, w)
    log_a = -LRU_C * r.astype(jnp.float32) * jax.nn.softplus(-lam.astype(jnp.float32))
    a = jnp.exp(log_a)
    mult = jnp.sqrt(-jnp.expm1(2.0 * log_a))
    b = mult * (i * x).astype(jnp.float32)
    _, h = lax.associative_scan(_lru_combine, (a, b), axis=1)
    return h.astype(x.dtype)

def second_inputs(seed: int = 0) -> dict:
    key = jax.random.key(seed)
    ks = jax.random.split(key, 24)
    f32 = jnp.float32
    L = DEPTH

    def nrm(k, shape, scale):
        return jax.random.normal(k, shape, f32) * scale

    x = jax.random.normal(ks[0], (BATCH, SEQ, D_MODEL), f32)
    norm1_g = 1.0 + nrm(ks[1], (L, D_MODEL), 0.05)
    w_in = nrm(ks[2], (L, D_MODEL, IN_COLS), D_MODEL ** -0.5)
    gm_v_g = 1.0 + nrm(ks[3], (L, GM_WIDTH), 0.05)
    gm_v_b = nrm(ks[4], (L, GM_WIDTH), 0.02)
    gm_ws = nrm(ks[5], (L, GM_HEADS, CHUNK, CHUNK), CHUNK ** -0.5)
    gm_bs = 1.0 + nrm(ks[6], (L, GM_HEADS, CHUNK), 0.1)
    lru_conv_w = nrm(ks[7], (L, LRU_CONV, LRU_WIDTH), LRU_CONV ** -0.5)
    lru_conv_b = nrm(ks[8], (L, LRU_WIDTH), 0.02)
    lru_wa = nrm(ks[9], (L, LRU_HEADS, LRU_BLOCK, LRU_BLOCK), LRU_BLOCK ** -0.5)
    lru_ba = nrm(ks[10], (L, LRU_HEADS, LRU_BLOCK), 0.02)
    lru_wx = nrm(ks[11], (L, LRU_HEADS, LRU_BLOCK, LRU_BLOCK), LRU_BLOCK ** -0.5)
    lru_bx = nrm(ks[12], (L, LRU_HEADS, LRU_BLOCK), 0.02)
    a_c = jax.random.uniform(ks[13], (L, LRU_WIDTH), f32, 0.9, 0.999)
    a_base = a_c ** (1.0 / LRU_C)
    lru_lambda = jnp.log(a_base) - jnp.log1p(-a_base)
    gm_out_g = 1.0 + nrm(ks[14], (L, GM_WIDTH), 0.05)
    lru_out_g = 1.0 + nrm(ks[15], (L, LRU_WIDTH), 0.05)
    w_out = nrm(ks[16], (L, D_MIX, D_MODEL), D_MIX ** -0.5)
    norm2_g = 1.0 + nrm(ks[17], (L, D_MODEL), 0.05)
    ffn_w_up = nrm(ks[18], (L, D_MODEL, 2 * D_FF_2), D_MODEL ** -0.5)
    ffn_conv_w = nrm(ks[19], (L, FFN_CONV, 2 * D_FF_2), FFN_CONV ** -0.5)
    ffn_conv_b = nrm(ks[20], (L, 2 * D_FF_2), 0.02)
    ffn_w_down = nrm(ks[21], (L, D_FF_2, D_MODEL), D_FF_2 ** -0.5)
    final_g = 1.0 + nrm(ks[22], (D_MODEL,), 0.05)
    return {
        "x": x, "norm1_g": norm1_g, "w_in": w_in,
        "gm_v_g": gm_v_g, "gm_v_b": gm_v_b, "gm_ws": gm_ws, "gm_bs": gm_bs,
        "lru_conv_w": lru_conv_w, "lru_conv_b": lru_conv_b,
        "lru_wa": lru_wa, "lru_ba": lru_ba, "lru_wx": lru_wx, "lru_bx": lru_bx,
        "lru_lambda": lru_lambda, "gm_out_g": gm_out_g, "lru_out_g": lru_out_g,
        "w_out": w_out, "norm2_g": norm2_g, "ffn_w_up": ffn_w_up,
        "ffn_conv_w": ffn_conv_w, "ffn_conv_b": ffn_conv_b, "ffn_w_down": ffn_w_down,
        "final_g": final_g,
    }

def second_block(x, norm1_g, w_in, gm_v_g, gm_v_b, gm_ws, gm_bs, lru_conv_w, lru_conv_b,
              lru_wa, lru_ba, lru_wx, lru_bx, lru_lambda, gm_out_g, lru_out_g, w_out,
              norm2_g, ffn_w_up, ffn_conv_w, ffn_conv_b, ffn_w_down, final_g):
    for l in range(DEPTH):
        h = _rmsnorm(x, norm1_g[l])
        p = jnp.einsum('bsd,de->bse', h, w_in[l])
        z_gm = p[..., :2 * GM_WIDTH]
        g_lru = p[..., 2 * GM_WIDTH:2 * GM_WIDTH + LRU_WIDTH]
        x_lru = p[..., 2 * GM_WIDTH + LRU_WIDTH:]
        y_gm = _spatial_gating(jax.nn.gelu(z_gm), gm_v_g[l], gm_v_b[l], gm_ws[l], gm_bs[l])
        xr = _causal_dwconv(x_lru, lru_conv_w[l], lru_conv_b[l])
        y_lru = _rg_lru(xr, lru_wa[l], lru_ba[l], lru_wx[l], lru_bx[l], lru_lambda[l])
        y_lru = y_lru * jax.nn.gelu(g_lru)
        y = jnp.concatenate([_rmsnorm(y_gm, gm_out_g[l]), _rmsnorm(y_lru, lru_out_g[l])], axis=-1)
        x = x + jnp.einsum('bse,ed->bsd', y, w_out[l])
        h = _rmsnorm(x, norm2_g[l])
        up = jnp.einsum('bsd,df->bsf', h, ffn_w_up[l])
        up = _causal_dwconv(up, ffn_conv_w[l], ffn_conv_b[l])
        gate, val = jnp.split(up, 2, axis=-1)
        x = x + jnp.einsum('bsf,fd->bsd', jax.nn.gelu(gate) * val, ffn_w_down[l])
    return _rmsnorm(x, final_g)


def setup_inputs(seed=0):
    out = dict(first_inputs(seed))
    for name, value in second_inputs(seed + 1).items():
        if name != "x":
            out[name + "_2"] = value
    return out


def reference(
    x, norm1_g, w_in, fox_f_bias, q_norm_g, k_norm_g, m_i_bias, m_f_bias, m_norm_g, w_proj_a,
    w_proj_m, w_out, norm2_g, w_up, conv_w, conv_b, w_down, norm1_g_2, w_in_2, gm_v_g_2,
    gm_v_b_2, gm_ws_2, gm_bs_2, lru_conv_w_2, lru_conv_b_2, lru_wa_2, lru_ba_2, lru_wx_2,
    lru_bx_2, lru_lambda_2, gm_out_g_2, lru_out_g_2, w_out_2, norm2_g_2, ffn_w_up_2,
    ffn_conv_w_2, ffn_conv_b_2, ffn_w_down_2, final_g_2,
):
    x = first_block(
        x, norm1_g, w_in, fox_f_bias, q_norm_g, k_norm_g, m_i_bias, m_f_bias, m_norm_g,
        w_proj_a, w_proj_m, w_out, norm2_g, w_up, conv_w, conv_b, w_down,
    )
    return second_block(
        x, norm1_g_2, w_in_2, gm_v_g_2, gm_v_b_2, gm_ws_2, gm_bs_2, lru_conv_w_2, lru_conv_b_2,
        lru_wa_2, lru_ba_2, lru_wx_2, lru_bx_2, lru_lambda_2, gm_out_g_2, lru_out_g_2, w_out_2,
        norm2_g_2, ffn_w_up_2, ffn_conv_w_2, ffn_conv_b_2, ffn_w_down_2, final_g_2,
    )


_drawn_inputs = setup_inputs


def setup_inputs(seed=0):
    import zlib

    import numpy as np

    out = dict(_drawn_inputs(seed))
    spreads = {}
    factors = {'q_norm_g': 2.674,
     'm_i_bias': 64.0,
     'conv_b': 2.728,
     'gm_v_g_2': 4.256,
     'gm_v_b_2': 28.201,
     'lru_ba_2': 28.783,
     'lru_bx_2': 8.0,
     'ffn_conv_b_2': 5.18,
     'gm_bs_2': 3.241}
    for name, (base, spread) in spreads.items():
        noise = np.random.default_rng([zlib.crc32(name.encode()), seed]).standard_normal(out[name].shape)
        drawn = base * np.exp(spread * noise) if base else spread * noise
        out[name] = __import__('jax').numpy.asarray(drawn.astype(out[name].dtype))
    for name, factor in factors.items():
        out[name] = (out[name] * factor).astype(out[name].dtype)
    return out
```

```python
from contextlib import ExitStack

import concourse.bass as bass
from concourse import mybir

F32 = mybir.dt.float32
F32R = mybir.dt.float32r
ALU = mybir.AluOpType
ACT = mybir.ActivationFunctionType
AX = mybir.AxisListType

P = 128
S = 256
D = 2048
KD = D // P
GROUP = 256
RING = 4
KT = 4
LOOKAHEAD = 3
EPS = 1e-6
LN_EPS = 1e-5

FOX_HEADS, FOX_HD = 8, 128
ML_HEADS, ML_DQK, ML_DV = 4, 128, 256
NG = FOX_HEADS + ML_HEADS
OFF_FQ, OFF_FK, OFF_FV = 0, 1024, 2048
OFF_FF = 3072
OFF_MQ = OFF_FF + FOX_HEADS
OFF_MK = OFF_MQ + 512
OFF_MV = OFF_MK + 512
OFF_MO = OFF_MV + 1024
OFF_MI = OFF_MO + 1024
OFF_MF = OFF_MI + ML_HEADS
OFF_GA = OFF_MF + ML_HEADS
OFF_GM = OFF_GA + D
FF1, FF2 = 5632, 6144
KT1 = [4] * 8 + [3] * 4
KT2 = [4] * 12
LRU_C = 8.0

VECTORS = [("norm1_g", 16), ("q_norm_g", 1), ("k_norm_g", 1), ("m_norm_g", 8), ("norm2_g", 16),
           ("conv_w", 3 * 88), ("conv_b", 88), ("norm1_g_2", 16), ("gm_v_g_2", 8), ("gm_v_b_2", 8),
           ("lru_conv_w_2", 32), ("lru_conv_b_2", 8), ("lru_ba_2", 8), ("lru_bx_2", 8),
           ("lru_lambda_2", 8), ("gm_out_g_2", 8), ("lru_out_g_2", 8), ("norm2_g_2", 16),
           ("ffn_conv_w_2", 3 * 96), ("ffn_conv_b_2", 96), ("final_g_2", 16)]
COL, _n = {}, 0
for _name, _tiles in VECTORS:
    COL[_name] = _n
    _n += _tiles
NVEC = _n


class Chain:

    def __init__(self, eng, sem):
        self.eng, self.sem, self.base, self.k, self.it, self.per = eng, sem, 0, 0, None, 0

    def mark(self, ins):
        ins.then_inc(self.sem, 1)
        self.k += 1

    def settle(self):
        n = self.base + self.k
        self.eng.wait_ge(self.sem, n if self.it is None else self.it * self.per + n)

    def enter(self, it, per):
        self.base, self.k, self.it, self.per = self.base + self.k, 0, it, per

    def leave(self, n):
        assert self.k == self.per, f"the loop's body marks {self.k}"
        self.base, self.k, self.it, self.per = self.base + n * self.per, 0, None, 0


def build(nc, w):
    stack = ExitStack()
    with stack:
        at = {}
        cursor = [16512]

        def here(name, shape, dt, offset=None):
            size = 4
            for n in shape[1:]:
                size *= n
            if offset is None:
                offset = cursor[0]
                cursor[0] += (size + 31) // 32 * 32
            at[name] = offset
            return nc.alloc_sbuf_tensor_at(name, shape, dt, offset=offset)

        X = here("X", [P, KD, S], F32)
        YHL = here("YHL", [P, KD, 2 * S], F32R)
        H = here("H", [P, 48, 2 * S], F32R)
        RAW = here("RAW", [P, RING, KT, GROUP], F32)
        HI = here("HI", [P, RING, KT, GROUP], F32R)
        LO = here("LO", [P, RING, KT, GROUP], F32R)
        VEC = here("VEC", [P, NVEC], F32)
        ONES = here("ONES", [P, P], F32)
        IDENT = here("IDENT", [P, P], F32)
        RSTD = here("RSTD", [P, S], F32)
        SQSUM = here("SQSUM", [P, 2, S], F32)
        QG = here("QG", [P, 1], F32)
        EPS1 = here("EPS1", [P, 1], F32)
        EPS5 = here("EPS5", [P, 1], F32)
        C8 = here("C8", [P, 8], F32)
        RCOL = here("RCOL", [P, 8], F32)
        WORK = cursor[0]
        assert WORK + 8224 <= 229368, WORK

        UP = here("UP", [P, 2, 2, S + 2], F32, WORK)
        YC = here("YC", [P, 4, S], F32, WORK + 4128)
        LG = here("LG", [P, 2, 384], F32, WORK)
        PTS = here("PTS", [P, 2, 384], F32, WORK + 3072)
        MASK = here("MASK", [P, 384], F32, WORK + 6144)
        CUM = here("CUM", [P, NG, 2], F32, WORK + 7680)
        NCUM = here("NCUM", [P, NG, 2], F32, WORK + 7776)
        MX = here("MX", [P, 2, 2], F32, WORK + 7872)
        NM = here("NM", [P, 2, 2], F32, WORK + 7904)
        RS = here("RS", [P, 2, 2], F32, WORK + 7936)
        EM = here("EM", [P, 2, 2], F32, WORK + 7968)
        SG = here("SG", [P, 2, 2, S], F32, WORK)
        T1 = here("T1", [P, 2, S], F32, WORK + 4096)
        T2 = here("T2", [P, 2, S], F32, WORK + 6144)
        XR = here("XR", [P, S], F32, WORK)
        RI = here("RI", [P, 2, S], F32, WORK + 1024)
        LA = here("LA", [P, S], F32, WORK + 3072)
        LT = here("LT", [P, S], F32, WORK + 4096)
        LM = here("LM", [P, S], F32, WORK + 5120)
        ZT = here("ZT", [P, 2, S], F32, WORK + 6144)

        AHL = H[:, 0:16]
        MHL = H[:, 16:32]
        M1 = at["H"] + 32 * 2048
        QT = here("QT", [P, 2, S], F32, M1)
        KTT = here("KTT", [P, 2, S], F32, M1 + 2048)
        VT = here("VT", [P, 2, 2, S], F32, M1 + 4096)
        SQ = here("SQ", [P, 2, 2, S], F32, M1 + 8192)
        RT = here("RT", [P, 2, 2, S], F32, M1 + 12288)
        DG = here("DG", [P, 4, 2, P], F32, M1 + 12288)
        VTOK = here("VTOK", [P, 2, 2, 256], F32, M1 + 16384)
        MO = here("MO", [P, 2, 2, S], F32, M1 + 20480)
        HM = here("HM", [P, 2, 2, S], F32, M1 + 24576)
        ROWS = here("ROWS", [NG, S], F32, M1 + 28672)
        RSEL = here("RSEL", [NG, 2, S], F32, M1 + 29696)
        TRI = here("TRI", [P, S], F32, M1 + 31744)
        XSQ = here("XSQ", [P, KD, S], F32, M1)
        WG = here("WG", [P, KD, 16], F32, M1 + 20480)
        WGH = here("WGH", [P, KD, 16], F32R, M1 + 21504)
        WGL = here("WGL", [P, KD, 16], F32R, M1 + 22528)
        GB = here("GB", [P, 16], F32, M1 + 23552)
        GZT = here("GZT", [P, 2, 16], F32, M1 + 24576)
        GA_ = here("GA_", [P, 2, 16], F32, M1 + 24704)
        GE = here("GE", [P, 2, 16], F32, M1 + 24832)
        LF = here("LF", [P, 2, NG], F32, M1 + 24960)
        NLF = here("NLF", [P, 2, NG], F32, M1 + 25088)
        GI = here("GI", [P, 2, NG], F32, M1 + 25216)
        SQQ = here("SQQ", [P, 4, S], F32, M1 + 25600)
        assert at["TRI"] + 1024 <= at["RAW"]

        M2 = at["H"] + 16 * 2048
        GZ = here("GZ", [P, 16, S], F32, M2)
        XL = here("XL", [P, 8, S + 3], F32, M2 + 16384)
        HL = here("HL", [P, 8, S], F32, M2 + 24704)
        GL = here("GL", [P, 8, S], F32, M2 + 32896)
        SQV = here("SQV", [P, 8, S], F32, M2 + 41088)
        WST = here("WST", [P, 8, P], F32, M2 + 49280)
        WAX = here("WAX", [P, 2, 2, P], F32, M2 + 53376)
        VNS = here("VNS", [P, 2, S], F32, M2 + 55424)
        VTK = here("VTK", [P, 2, 2, P], F32, M2 + 57472)
        BSR = here("BSR", [1, 8 * P], F32, M2 + 59520)
        MU = here("MU", [P, S], F32, M2 + 63616)
        assert M2 + 64640 <= at["RAW"]

        PS = stack.enter_context(nc.psum_tensor("PS", [P, 8, 512], F32))

        def acc(buf):
            return PS[:, 2 * buf:2 * buf + 2, :].rearrange("p m (h n) -> p m n h", h=2)

        def sem(name):
            return stack.enter_context(nc.semaphore(name))

        raw_landed = [sem(f"raw_landed{i}") for i in range(RING)]
        hi_ready, lo_ready = sem("hi_ready"), sem("lo_ready")
        chunk_used = sem("chunk_used")
        acc_evacuated = sem("acc_evacuated")
        x_landed = [sem(f"x_landed{i}") for i in range(4)]
        vec_landed, gate_w_landed, gate_b_landed = sem("vec_landed"), sem("gate_w_landed"), sem("gate_b_landed")
        consts_made, ident_made = sem("consts_made"), sem("ident_made")
        x_squared, sq_summed, norm_acc, norm_root = sem("x_squared"), sem("sq_summed"), sem("norm_acc"), sem("norm_root")
        x_added, nhi_ready, nlo_ready, scaled = sem("x_added"), sem("nhi_ready"), sem("nlo_ready"), sem("scaled")
        rstd_ready, sq_added = sem("rstd_ready"), sem("sq_added")
        rcol_ready, dg_ready = sem("rcol_ready"), sem("dg_ready")
        col_sums, col_roots = sem("col_sums"), sem("col_roots")
        dve_own, act_own, pool_own = sem("dve_own"), sem("act_own"), sem("pool_own")
        wg_hi, wg_lo, gates_acc, gate_abs, gate_exp, gate_ln, logf_ready = [
            sem(n) for n in ("wg_hi", "wg_lo", "gates_acc", "gate_abs", "gate_exp", "gate_ln", "logf_ready")]
        rsel_ready = sem("rsel_ready")
        cum_acc, cum_ready = sem("cum_acc"), sem("cum_ready")
        sq_ready, sums_ready, qk_normed = sem("sq_ready"), sem("sums_ready"), sem("qk_normed")
        logits_ready, negmax_ready, exp_ready, prob_ready = [
            sem(n) for n in ("logits_ready", "negmax_ready", "exp_ready", "prob_ready")]
        vtr_ready, vtok_ready, ptr_ready, pts_ready = [
            sem(n) for n in ("vtr_ready", "vtok_ready", "ptr_ready", "pts_ready")]
        pv_ready, ahi_ready, alo_ready = sem("pv_ready"), sem("ahi_ready"), sem("alo_ready")
        m_rows, m_qk, m_negmax, m_exp, m_prob = [
            sem(n) for n in ("m_rows", "m_qk", "m_negmax", "m_exp", "m_prob")]
        m_vtr, m_vtok, m_ptr, m_pts, m_pv, m_hm, m_gate, m_sq, m_sums, m_rt, m_out, m_ahi, m_alo = [
            sem(n) for n in ("m_vtr", "m_vtok", "m_ptr", "m_pts", "m_pv", "m_hm", "m_gate", "m_sq", "m_sums",
                             "m_rt", "m_out", "m_ahi", "m_alo")]
        sg_ready, merged_ready, mhi_ready, mlo_ready = [
            sem(n) for n in ("sg_ready", "merged_ready", "mhi_ready", "mlo_ready")]
        tap_ready, conv_ready, gate_act, hid_ready, hhi_ready, hlo_ready = [
            sem(n) for n in ("tap_ready", "conv_ready", "gate_act", "hid_ready", "hhi_ready", "hlo_ready")]
        c8_exp, c8_ln, c8_ready, c8_abs = sem("c8_exp"), sem("c8_ln"), sem("c8_ready"), sem("c8_abs")
        xl_ready, xr_tap, xr_ready, wax_landed, lru_acc, lru_gates, lru_th, lru_q, lru_mult, lru_done = [
            sem(n) for n in ("xl_ready", "xr_tap", "xr_ready", "wax_landed", "lru_acc", "lru_gates", "lru_th",
                             "lru_q", "lru_mult", "lru_done")]
        gelu_done, ws_landed, ws_masked, bs_landed = sem("gelu_done"), sem("ws_landed"), sem("ws_masked"), sem("bs_landed")
        ln_sum, ln_acc, ln_centered, ln_sq, ln_root, ln_ready = [
            sem(n) for n in ("ln_sum", "ln_acc", "ln_centered", "ln_sq", "ln_root", "ln_ready")]
        vn_ready, vtk_acc, vtk_ready, mix_acc, mixed_ready = [
            sem(n) for n in ("vn_ready", "vtk_acc", "vtk_ready", "mix_acc", "mixed_ready")]
        f_in, f_sq, f_sum, f_acc, f_root, f_scaled, f_hi, f_lo = [
            sem(n) for n in ("f_in", "f_sq", "f_sum", "f_acc", "f_root", "f_scaled", "f_hi", "f_lo")]
        out_ready, out_done = sem("out_ready"), sem("out_done")

        C_FOX, G_FOX = 0, 0
        C_ML, G_ML = C_FOX + 48, G_FOX + 12
        C_MG, G_MG = C_ML + 48, G_ML + 12
        C_OUT, G_OUT = C_MG + 96, G_MG + 32
        C_UP, G_UP = C_OUT + 32, G_OUT + 8
        C_DN, G_DN = C_UP + 8 * 22, G_UP + 2 * 22
        C_XL, G_XL = C_DN + 96, G_DN + 8
        C_ZU, G_ZU = C_XL + 16, G_XL + 4
        C_GL, G_GL = C_ZU + 32, G_ZU + 8
        C_O2, G_O2 = C_GL + 16, G_GL + 4
        C_U2, G_U2 = C_O2 + 32, G_O2 + 8
        C_D2, G_D2 = C_U2 + 8 * 24, G_U2 + 2 * 24

        Z_FOX, Z_ML, Z_MG, Z_UP = 0, 12, 24, 40
        Z_XL = Z_UP + 2 * 22
        Z_ZU, Z_GL, Z_U2 = Z_XL + 4, Z_XL + 12, Z_XL + 16

        FOX_OFFS = [OFF_FQ, OFF_FK, OFF_FV]

        def ml_cols(i):
            return [OFF_MQ + 256 * i, OFF_MK + 256 * i, OFF_MV + 512 * i, OFF_MV + 512 * i + 256,
                    OFF_MO + 512 * i, OFF_MO + 512 * i + 256]

        def at_tile(k, base=0):
            return bass.ds(k + base, 1)

        block = stack.enter_context(nc.Block())

        @block.sync
        def _(sp):
            def load(c, j, src, row, kts, col):
                sp.wait_ge(lo_ready, c + (j + 1))
                sp.dma_start(RAW[:, j % RING, 0:kts, :],
                             src[row:row + kts * P, bass.ds(col, GROUP)].rearrange("(k p) n -> p k n", p=P)
                             ).then_inc(raw_landed[j % RING], 16)

            def load_group(c, j, src, col, kts=(4, 4, 4, 4)):
                row = 0
                for n, k in enumerate(kts):
                    load(c, j + n, src, row, k, col)
                    row += k * P

            sp.sem_inc(lo_ready, RING)
            with sp.Fori(1, 5) as i:
                for n, off in enumerate(FOX_OFFS):
                    load_group(i * 12 + (C_FOX - 12), 4 * n, w["w_in"], i * 256 + (off - 256))
            for i in range(2):
                for n, off in enumerate(ml_cols(i)):
                    load_group(C_ML + 24 * i, 4 * n, w["w_in"], off)
            with sp.Fori(1, 9) as i:
                c = i * 12 + (C_MG - 12)
                load_group(c, 0, w["w_in"], i * 256 + (OFF_GA - 256))
                load_group(c, 4, w["w_in"], i * 256 + (OFF_GM - 256))
                load_group(c, 8, w["w_proj_a"], i * 256 - 256, (4, 4))
                load_group(c, 10, w["w_proj_m"], i * 256 - 256, (4, 4))

            def square(c, src, kts=(4, 4, 4, 4)):
                per = 2 * len(kts)
                with sp.Fori(1, 5) as i:
                    for n in range(2):
                        load_group(i * per + (c - per), n * len(kts), src, i * 512 + (n * 256 - 512), kts)

            def up(c, src, ff):
                with sp.Fori(1, ff // GROUP + 1) as i:
                    load_group(i * 8 + (c - 8), 0, src, i * 256 - 256)
                    load_group(i * 8 + (c - 8), 4, src, i * 256 + (ff - 256))

            square(C_OUT, w["w_out"])
            up(C_UP, w["w_up"], FF1)
            square(C_DN, w["w_down"], KT1)
            with sp.Fori(1, 3) as i:
                for n in range(2):
                    load_group(i * 8 + (C_XL - 8), 4 * n, w["w_in_2"], i * 512 + (3072 + 256 * n - 512))
            with sp.Fori(1, 5) as i:
                for n in range(2):
                    load_group(i * 8 + (C_ZU - 8), 4 * n, w["w_in_2"], i * 512 + (256 * n - 512))
            with sp.Fori(1, 3) as i:
                for n in range(2):
                    load_group(i * 8 + (C_GL - 8), 4 * n, w["w_in_2"], i * 512 + (2048 + 256 * n - 512))
            square(C_O2, w["w_out_2"])
            up(C_U2, w["ffn_w_up_2"], FF2)
            square(C_D2, w["ffn_w_down_2"], KT2)
            for q in range(4):
                sp.wait_ge(out_ready, 4 * q + 4)
                sp.dma_start(w["out"][:, 4 * q:4 * q + 4, :], X[:, 4 * q:4 * q + 4, :]).then_inc(out_done, 16)
            sp.wait_ge(out_done, 64)

        @block.gpsimd
        def _(pool):
            own = Chain(pool, pool_own)
            pool.dma_start(WG[:, :, :], w["w_gate"]).then_inc(gate_w_landed, 16)
            pool.dma_start(VEC[:, :], w["vec"]).then_inc(vec_landed, 16)
            pool.dma_start(GB[:, :], w["gate_b"].to_broadcast([P, 16])).then_inc(gate_b_landed, 16)
            pool.memset(ONES[:, :], 1.0).then_inc(consts_made, 1)
            pool.memset(EPS1[:, :], EPS).then_inc(consts_made, 1)
            pool.memset(EPS5[:, :], LN_EPS).then_inc(consts_made, 1)
            own.mark(pool.memset(IDENT[:, :], 0.0))
            own.mark(pool.memset(TRI[:, :], 1.0))
            own.settle()
            pool.affine_select(out=IDENT[:, :], in_=IDENT[:, :], compare_op=ALU.not_equal, fill=1.0, base=0,
                               pattern=[[-1, P]], channel_multiplier=1).then_inc(ident_made, 1)
            pool.affine_select(out=TRI[:, :], in_=TRI[:, :], compare_op=ALU.is_ge, fill=0.0, base=0,
                               pattern=[[1, S]], channel_multiplier=-1).then_inc(ident_made, 1)
            own.mark(pool.memset(MASK[:, :], 0.0))
            own.settle()
            for a in (0, 256):
                pool.affine_select(out=MASK[:, a:a + P], in_=MASK[:, a:a + P], compare_op=ALU.is_ge, fill=-3.0e38,
                                   base=0, pattern=[[-1, P]], channel_multiplier=1).then_inc(ident_made, 1)
            pool.wait_ge(chunk_used, C_XL + RING)
            pool.dma_start(WST[:, :, :], w["gm_ws_2"]).then_inc(ws_landed, 16)
            pool.dma_start(BSR[:, :], w["gm_bs_2"]).then_inc(bs_landed, 16)
            pool.wait_ge(ws_landed, 16)
            pool.affine_select(out=WST[:, :, :], in_=WST[:, :, :], compare_op=ALU.is_ge, fill=0.0, base=0,
                               pattern=[[0, 8], [1, P]], channel_multiplier=-1).then_inc(ws_masked, 1)
            pool.sem_inc(lru_acc, 2)
            with pool.Fori(0, 4) as i:
                for n in range(2):
                    pool.wait_ge(lru_acc, i * 2 + (n + 1))
                    pool.dma_start(WAX[:, n, 0, :], w["lru_wa_2"][:, bass.ds(i * 2 + n, 1), :]
                                   ).then_inc(wax_landed, 16)
                    pool.dma_start(WAX[:, n, 1, :], w["lru_wx_2"][:, bass.ds(i * 2 + n, 1), :]
                                   ).then_inc(wax_landed, 16)
                    pool.wait_ge(wax_landed, i * 64 + 32 * (n + 1))

        @block.tensor
        def _(pe):
            def group(c, j, g, buf, moving, kts=(4, 4, 4, 4), strong=False, ready=None, hooks=None):
                pe.wait_ge(acc_evacuated, g + (2 if strong else 1))
                k, total = 0, sum(kts)
                for n, kt in enumerate(kts):
                    if ready is not None:
                        ready(n, k + kt)
                    pe.wait_ge(lo_ready, c + (j + n + 1 + RING))
                    slot = (j + n) % RING
                    for t in range(kt):
                        for m in range(2):
                            cols = slice(m * P, m * P + P)
                            nc.tensor.matmul(PS[:, 2 * buf + m, :], HI[:, slot, t, cols], moving[:, k, :],
                                             start=(k == 0), stop=False)
                            mm = nc.tensor.matmul(PS[:, 2 * buf + m, 0:S], LO[:, slot, t, cols],
                                                  moving[:, k, 0:S], start=False, stop=(k == total - 1))
                        k += 1
                    mm.then_inc(chunk_used, 1)
                    for hook in (hooks or {}).get(n, ()):
                        hook()

            def partition_sums(out, parts, signal):
                for n, part in enumerate(parts):
                    mm = nc.tensor.matmul(out, ONES[:, :], part, start=(n == 0), stop=(n == len(parts) - 1))
                mm.then_inc(signal, 1)

            def norm_sums(n):
                pe.wait_ge(sq_added, 8 * n)
                partition_sums(PS[:, 7, 0:S], [SQSUM[:, m, :] for m in range(2)], norm_acc)

            def normed(n):
                return lambda _, k: pe.wait_ge(nlo_ready, KD * n + k)

            pe.sem_inc(chunk_used, RING)

            def first_norm_sums():
                pe.wait_ge(consts_made, 3)
                for q in range(4):
                    pe.wait_ge(sq_summed, q + 1)
                    mm = nc.tensor.matmul(PS[:, 7, 0:S], ONES[:, :], SQQ[:, q, :], start=(q == 0), stop=(q == 3))
                mm.then_inc(norm_acc, 1)

            def gate_products():
                pe.wait_ge(wg_lo, 1)
                for tb in range(2):
                    for k in range(KD):
                        hi = YHL[:, k, tb * P:tb * P + P]
                        lo = YHL[:, k, S + tb * P:S + tb * P + P]
                        nc.tensor.matmul(PS[:, 4 + tb, 0:16], hi, WGH[:, k, :], start=(k == 0), stop=False)
                        nc.tensor.matmul(PS[:, 4 + tb, 0:16], hi, WGL[:, k, :], start=False, stop=False)
                        mm = nc.tensor.matmul(PS[:, 4 + tb, 0:16], lo, WGH[:, k, :], start=False,
                                              stop=(k == KD - 1))
                mm.then_inc(gates_acc, 1)

            def rstd_columns():
                pe.wait_ge(rstd_ready, 1)
                for tb in range(2):
                    mm = nc.tensor.matmul(PS[:, 6, tb:tb + 1], RSTD[0:1, tb * P:tb * P + P], ONES[0:1, 0:1],
                                          start=True, stop=True)
                mm.then_inc(rcol_ready, 1)

            def cumulate():
                pe.wait_ge(logf_ready, 3)
                pe.wait_ge(ident_made, 2)
                nc.tensor.matmul(PS[:, 6, 0:NG], TRI[:, 0:P], LF[:, 0, :], start=True, stop=True)
                nc.tensor.matmul(PS[:, 6, 16:16 + NG], TRI[:, P:S], LF[:, 0, :], start=True, stop=False)
                nc.tensor.matmul(PS[:, 6, 16:16 + NG], TRI[:, 0:P], LF[:, 1, :], start=False, stop=True)
                nc.tensor.matmul(PS[0:NG, 7, 0:S], NLF[:, 0, :], TRI[:, :], start=True, stop=False)
                nc.tensor.matmul(PS[0:NG, 7, P:S], NLF[:, 1, :], TRI[:, 0:P], start=False, stop=False)
                nc.tensor.matmul(PS[0:NG, 7, 0:P], GI[:, 0, :], IDENT[:, :], start=False, stop=False)
                nc.tensor.matmul(PS[0:NG, 7, P:S], GI[:, 1, :], IDENT[:, :], start=False, stop=True
                                 ).then_inc(cum_acc, 1)

            def add_logits(m, bank, signal):
                for out, qs, ks in ((PS[:, bank, 0:P], slice(0, P), slice(0, P)),
                                    (PS[:, bank, P:384], slice(P, S), slice(0, S))):
                    nc.tensor.matmul(out, QT[:, m, qs], KTT[:, m, ks], start=True, stop=False)
                    mm = nc.tensor.matmul(out, ONES[0:NG, :], RSEL[:, m, ks], start=False, stop=True)
                mm.then_inc(signal, 1)

            def transpose_v(m, bank, signal):
                for tb in range(2):
                    for t in range(2):
                        mm = nc.tensor.transpose(PS[:, bank, tb * 256 + t * P:tb * 256 + t * P + P],
                                                 VT[:, m, t, tb * P:tb * P + P], IDENT[:, :])
                mm.then_inc(signal, 1)

            def transpose_p(m, bank, signal):
                for b in range(3):
                    mm = nc.tensor.transpose(PS[:, bank, b * P:b * P + P], LG[:, m, b * P:b * P + P], IDENT[:, :])
                mm.then_inc(signal, 1)

            def weigh_v(out0, vm, cols, pm):
                nc.tensor.matmul(out0, VTOK[:, vm, 0, cols], PTS[:, pm, 0:S], start=True, stop=False)
                return nc.tensor.matmul(out0[:, P:S], VTOK[:, vm, 1, cols], PTS[:, pm, S:384], start=False, stop=True)

            def fox_sums(i, first):
                def hook():
                    if not first:
                        pe.wait_ge(vtok_ready, i)
                    else:
                        cumulate()
                        pe.wait_ge(cum_ready, 2)
                    for n in range(2):
                        pe.wait_ge(sq_ready, i * 2 + (n + 1))
                        for m in range(2):
                            for tb in range(2):
                                j = 4 * n + 2 * m + tb
                                mm = nc.tensor.matmul(PS[:, 6, j:j + 1], SQ[:, n, m, tb * P:tb * P + P],
                                                      ONES[:, 0:1], start=True, stop=True)
                    mm.then_inc(col_sums, 1)
                return hook

            def fox_spread(i, first):
                def hook():
                    pe.wait_ge(dg_ready, i + 1)
                    if not first:
                        pe.wait_ge(alo_ready, i)
                    for n in range(2):
                        mm = nc.tensor.matmul(PS[:, 6 + n, :], ONES[:, :], DG[:, 2 * n:2 * n + 2, :, :],
                                              start=True, stop=True)
                    mm.then_inc(sums_ready, 1)
                return hook

            def fox_logits(i, first):
                def hook():
                    pe.wait_ge(qk_normed, i + 1)
                    if not first:
                        pe.wait_ge(pts_ready, i * 2)
                    for m in range(2):
                        add_logits(m, 4 + m, logits_ready)
                return hook

            def fox_transposes(i):
                def hook():
                    pe.wait_ge(scaled, i * 3 + (Z_FOX + 3))
                    transpose_v(0, 6, vtr_ready)
                    for m in range(2):
                        pe.wait_ge(prob_ready, i * 2 + (m + 1))
                        transpose_p(m, 4 + m, ptr_ready)
                return hook

            def fox_weigh(i):
                def hook():
                    pe.wait_ge(vtok_ready, i + 1)
                    pe.wait_ge(pts_ready, i * 2 + 2)
                    for m in range(2):
                        mm = weigh_v(PS[:, 7, m * S:m * S + S], 0, slice(m * P, m * P + P), m)
                    mm.then_inc(pv_ready, 1)
                return hook

            def fox(i, first):
                c, g = C_FOX + i * 12, G_FOX + i * 3
                if first:
                    group(c, 0, g, 0, YHL, ready=normed(0), hooks={3: [first_norm_sums, gate_products]})
                    group(c, 4, g + 1, 1, YHL, hooks={1: [rstd_columns]})
                else:
                    group(c, 0, g, 0, YHL, strong=True, hooks={3: [fox_transposes(i - 1)]})
                    group(c, 4, g + 1, 1, YHL, hooks={1: [fox_weigh(i - 1)]})
                group(c, 8, g + 2, 0, YHL, hooks={0: [fox_sums(i, first)], 2: [fox_spread(i, first)],
                                                  3: [fox_logits(i, first)]})

            fox(0, True)
            with pe.Fori(0, 3) as i:
                fox(i + 1, False)

            def ml_scores(i):
                def hook():
                    pe.wait_ge(scaled, Z_ML + 6 * i + 2)
                    if i == 0:
                        pe.wait_ge(alo_ready, 4)
                    else:
                        pe.wait_ge(m_rt, 2 * i)
                        pe.wait_ge(m_hm, 2 * i)
                    pe.wait_ge(rsel_ready, 2 * (4 + i) + 2)
                    for m in range(2):
                        for out, ks in ((PS[:, 4 + m, 0:P], slice(0, P)), (PS[:, 4 + m, P:384], slice(0, S))):
                            mm = nc.tensor.matmul(out, ONES[0:NG, :], RSEL[:, m, ks], start=True, stop=True)
                        mm.then_inc(m_rows, 1)
                        for out, qs, ks in ((PS[:, 6 + m, 0:P], slice(0, P), slice(0, P)),
                                            (PS[:, 6 + m, P:384], slice(P, S), slice(0, S))):
                            mm = nc.tensor.matmul(out, QT[:, m, qs], KTT[:, m, ks], start=True, stop=True)
                        mm.then_inc(m_qk, 1)
                return hook

            def ml_transposes(i, m):
                def hook():
                    pe.wait_ge(scaled, Z_ML + 6 * i + 3 + m)
                    pe.wait_ge(m_prob, 2 * i + m + 1)
                    transpose_v(m, 4 + m, m_vtr)
                    transpose_p(m, 6 + m, m_ptr)
                return hook

            def ml_weigh(i, m):
                def hook():
                    pe.wait_ge(m_vtok, 2 * i + m + 1)
                    pe.wait_ge(m_pts, 2 * i + m + 1)
                    for t in range(2):
                        mm = weigh_v(PS[:, 4 + m, t * S:t * S + S], m, slice(t * P, t * P + P), m)
                    mm.then_inc(m_pv, 1)
                return hook

            def ml_sums(i):
                def hook():
                    for m in range(2):
                        pe.wait_ge(m_sq, 2 * i + m + 1)
                        partition_sums(PS[:, 6 + m, 0:S], [SQ[:, m, t, :] for t in range(2)], m_sums)
                return hook

            for i in range(2):
                c, g = C_ML + 24 * i, G_ML + 6 * i
                group(c, 0, g, 1, YHL, hooks={3: [fox_transposes(3)]} if i == 0 else {2: [ml_sums(0)]})
                group(c, 4, g + 1, 0, YHL, hooks={1: [fox_weigh(3)]} if i == 0 else None)
                group(c, 8, g + 2, 1, YHL, hooks={1: [ml_scores(i)]})
                group(c, 12, g + 3, 0, YHL, hooks={2: [ml_transposes(i, 0)]})
                group(c, 16, g + 4, 1, YHL, hooks={1: [ml_weigh(i, 0)], 2: [ml_transposes(i, 1)]})
                group(c, 20, g + 5, 0, YHL, hooks={1: [ml_weigh(i, 1)]})

            def merge(i, first):
                c, g = C_MG + i * 12, G_MG + i * 4
                group(c, 0, g, 1, YHL, hooks={2: [ml_sums(1)]} if first else None)
                group(c, 4, g + 1, 0, YHL)
                if first:
                    pe.wait_ge(alo_ready, 4)
                    pe.wait_ge(m_alo, 4)
                group(c, 8, g + 2, 1, AHL[:, 0:8], (4, 4))
                group(c, 10, g + 3, 0, AHL[:, 8:16], (4, 4))

            merge(0, True)
            with pe.Fori(0, 7) as i:
                merge(i + 1, False)

            def square(c0, g0, moving, kts, ready):
                with pe.Fori(0, 4) as i:
                    for n in range(2):
                        group(c0 + i * (2 * len(kts)), n * len(kts), g0 + i * 2 + n, 1 - n, moving, kts,
                              ready=ready if n == 0 else None)

            def up(c0, g0, ff, n):
                group(c0, 0, g0, 1, YHL, ready=normed(n), hooks={1: [lambda: norm_sums(n)]})
                group(c0, 4, g0 + 1, 0, YHL)
                with pe.Fori(1, ff // GROUP) as i:
                    group(c0 + i * 8, 0, g0 + i * 2, 1, YHL)
                    group(c0 + i * 8, 4, g0 + i * 2 + 1, 0, YHL)

            K4 = (4, 4, 4, 4)
            square(C_OUT, G_OUT, MHL, K4, lambda _, k: pe.wait_ge(mlo_ready, k // 2))
            up(C_UP, G_UP, FF1, 1)
            square(C_DN, G_DN, H, KT1, lambda _, k: pe.wait_ge(hlo_ready, (k + 1) // 2))

            group(C_XL, 0, G_XL, 1, YHL, ready=normed(2), hooks={1: [lambda: norm_sums(2)]})
            group(C_XL, 4, G_XL + 1, 0, YHL)
            group(C_XL, 8, G_XL + 2, 1, YHL)
            group(C_XL, 12, G_XL + 3, 0, YHL)

            def lru_gate_products(k, n):
                def hook():
                    pe.wait_ge(wax_landed, k * 32 + 32)
                    pe.wait_ge(xr_ready, k * 3 + 3)
                    pe.wait_ge(lru_gates, k * 2 + 1)
                    for a in range(2):
                        mm = nc.tensor.matmul(PS[:, 4, a * S:a * S + S], WAX[:, n, a, :], XR[:, :],
                                              start=True, stop=True)
                    mm.then_inc(lru_acc, 1)
                return hook

            pe.sem_inc(lru_gates, 1)
            with pe.Fori(0, 4) as i:
                for n in range(2):
                    group(C_ZU + i * 8, 4 * n, G_ZU + i * 2 + n, 1 - n, YHL,
                          hooks={3: [lru_gate_products(i * 2 + n, n)]})

            for n in range(2):
                pe.wait_ge(ln_sum, n + 1)
                partition_sums(PS[:, 5, n * S:n * S + S], [SQSUM[:, n, :]], ln_acc)

            def turn_v(j):
                def hook():
                    pe.wait_ge(vn_ready, j * 2 + 2)
                    for m in range(2):
                        for b in range(2):
                            mm = nc.tensor.transpose(PS[:, 6, (2 * m + b) * P:(2 * m + b) * P + P],
                                                     VNS[:, m, b * P:b * P + P], IDENT[:, :])
                    mm.then_inc(vtk_acc, 1)
                return hook

            def mix(j):
                def hook():
                    pe.wait_ge(vtk_ready, j + 1)
                    pe.wait_ge(mixed_ready, j + 1)
                    for m in range(2):
                        for b in range(2):
                            out = PS[:, 7, m * S + b * P:m * S + b * P + P]
                            nc.tensor.matmul(out, VTK[:, m, b, :], WST[:, bass.ds(j * 2 + m, 1), :],
                                             start=True, stop=False)
                            mm = nc.tensor.matmul(out, ONES[0:1, :], BSR[0:1, bass.ds(j * (2 * P) + m * P, P)],
                                                  start=False, stop=True)
                    mm.then_inc(mix_acc, 1)
                return hook

            pe.sem_inc(mixed_ready, 1)
            pe.sem_inc(vtk_acc, 1)
            pe.wait_ge(ws_masked, 1)
            pe.wait_ge(bs_landed, 16)
            with pe.Fori(0, 2) as i:
                for n in range(2):
                    group(C_GL + i * 8, 4 * n, G_GL + i * 2 + n, 1 - n, YHL,
                          hooks={2: [turn_v(i * 2 + n)], 3: [mix(i * 2 + n)]})

            for n in range(2):
                pe.wait_ge(f_sum, n + 1)
                partition_sums(PS[:, 4 + n, 0:S], [SQSUM[:, n, :]], f_acc)

            square(C_O2, G_O2, AHL, K4, lambda _, k: pe.wait_ge(f_lo, k))
            up(C_U2, G_U2, FF2, 3)
            square(C_D2, G_D2, H, KT2, lambda _, k: pe.wait_ge(hlo_ready, 22 + (k + 1) // 2))
            norm_sums(4)

        @block.scalar
        def _(act):
            def hi(c, j, kt=4):
                s = j % RING
                act.wait_ge(raw_landed[s], c * 4 + 16 * (j // RING + 1))
                act.wait_ge(chunk_used, c + (j + 1))
                nc.scalar.activation(HI[:, s, 0:kt, :], RAW[:, s, 0:kt, :], ACT.Copy).then_inc(hi_ready, 1)

            def splits(c, a, b, kts=()):
                for j in range(a, b):
                    hi(c, j, kts[j] if j < len(kts) else 4)

            def norm_root_of(n):
                act.wait_ge(norm_acc, n + 1)
                nc.scalar.activation(RSTD[:, :], PS[:, 7, 0:S], ACT.Sqrt, bias=EPS1[:, :], scale=1.0 / D
                                     ).then_inc(norm_root, 1)

            def gain_hi(name, k, vk):
                nc.scalar.activation(YHL[:, at_tile(k), 0:S], X[:, at_tile(k), :], ACT.Copy,
                                     scale=VEC[:, at_tile(vk, COL[name])]).then_inc(nhi_ready, 1)

            for q in range(4):
                nc.scalar.dma_start(X[:, 4 * q:4 * q + 4, :], w["x"][:, 4 * q:4 * q + 4, :]).then_inc(x_landed[q], 16)
            act.wait_ge(vec_landed, 16)
            for q in range(4):
                act.wait_ge(x_landed[q], 16)
                for k in range(4 * q, 4 * q + 4):
                    gain_hi("norm1_g", k, k)
                if q < 3:
                    splits(C_FOX, q, q + 1)
                nc.scalar.activation(XSQ[:, 4 * q:4 * q + 4, :], X[:, 4 * q:4 * q + 4, :], ACT.Square
                                     ).then_inc(x_squared, 1)
            act.wait_ge(gate_w_landed, 16)
            nc.scalar.activation(WGH[:, :, :], WG[:, :, :], ACT.Copy).then_inc(wg_hi, 1)
            splits(C_FOX, 3, 4)
            act.wait_ge(consts_made, 3)
            norm_root_of(0)
            splits(C_FOX, 4, 5)

            def gate_logs():
                act.wait_ge(gate_abs, 1)
                nc.scalar.activation(GE[:, :, :], GA_[:, :, :], ACT.Exp, scale=-1.0).then_inc(gate_exp, 1)
                act.wait_ge(gate_exp, 1)
                nc.scalar.activation(GE[:, :, :], GE[:, :, :], ACT.Ln, bias=ONES[:, 0:1]).then_inc(gate_ln, 1)

            def exps(src, m, n, signal, sums):
                for b, cols in enumerate((slice(0, P), slice(P, 384))):
                    ins = nc.scalar.activation(LG[:, m, cols], LG[:, m, cols], ACT.Exp, bias=NM[:, m, b:b + 1],
                                               **({"accum_out": RS[:, m, b:b + 1]} if sums else {}))
                    ins.then_inc(signal, 1)

            def fox_copies(i):
                act.wait_ge(vtr_ready, i + 1)
                nc.scalar.activation(VTOK[:, 0, :, :], PS[:, 6, :].rearrange("p (b n) -> p b n", b=2), ACT.Copy
                                     ).then_inc(vtok_ready, 1)
                for m in range(2):
                    act.wait_ge(ptr_ready, i * 2 + (m + 1))
                    nc.scalar.activation(PTS[:, m, :], PS[:, 4 + m, 0:384], ACT.Copy).then_inc(pts_ready, 1)

            def fox_out_hi(i):
                act.wait_ge(pv_ready, i + 1)
                nc.scalar.activation(AHL[:, bass.ds(i * 2, 2), 0:S], PS[:, 7, :].rearrange("p (m n) -> p m n", m=2),
                                     ACT.Copy).then_inc(ahi_ready, 1)

            def fox(i, first):
                c = C_FOX + i * 12
                splits(c, 5, 7)
                act.wait_ge(scaled, i * 3 + (Z_FOX + 1))
                nc.scalar.activation(SQ[:, 0, :, :], QT[:, :, :], ACT.Square).then_inc(sq_ready, 1)
                if not first:
                    fox_copies(i - 1)
                splits(c, 7, 11)
                if not first:
                    fox_out_hi(i - 1)
                act.wait_ge(scaled, i * 3 + (Z_FOX + 2))
                nc.scalar.activation(SQ[:, 1, :, :], KTT[:, :, :], ACT.Square).then_inc(sq_ready, 1)
                if first:
                    gate_logs()
                splits(c, 11, 12)
                act.wait_ge(col_sums, i + 1)
                nc.scalar.activation(RCOL[:, :], PS[:, 6, 0:8], ACT.Sqrt, bias=EPS1[:, :], scale=1.0 / FOX_HD
                                     ).then_inc(col_roots, 1)
                splits(c, 12, 15)
                for m in range(2):
                    act.wait_ge(negmax_ready, i * 2 + (m + 1))
                    exps(LG, m, None, exp_ready, True)
                splits(c, 15, 17)

            fox(0, True)
            with act.Fori(0, 3) as i:
                fox(i + 1, False)

            def ml_exps(i, m):
                act.wait_ge(m_negmax, 2 * i + m + 1)
                exps(LG, m, None, m_exp, False)
                nc.scalar.activation(EM[:, m, :], NM[:, m, :], ACT.Exp).then_inc(m_exp, 1)

            def ml_copies(i, m):
                act.wait_ge(m_vtr, 2 * i + m + 1)
                nc.scalar.activation(VTOK[:, m, :, :], PS[:, 4 + m, :].rearrange("p (b n) -> p b n", b=2), ACT.Copy
                                     ).then_inc(m_vtok, 1)
                act.wait_ge(m_ptr, 2 * i + m + 1)
                nc.scalar.activation(PTS[:, m, :], PS[:, 6 + m, 0:384], ACT.Copy).then_inc(m_pts, 1)

            def ml_roots(i):
                for m in range(2):
                    act.wait_ge(m_sums, 2 * i + m + 1)
                    nc.scalar.activation(RT[:, m, 0, :], PS[:, 6 + m, 0:S], ACT.Sqrt, bias=EPS1[:, :],
                                         scale=1.0 / ML_DV).then_inc(m_rt, 1)

            def ml_out_hi(i):
                for m in range(2):
                    act.wait_ge(m_out, 2 * i + m + 1)
                    nc.scalar.activation(AHL[:, 8 + 4 * i + 2 * m:10 + 4 * i + 2 * m, 0:S], HM[:, m, :, :],
                                         ACT.Copy).then_inc(m_ahi, 1)

            for i in range(2):
                c = C_ML + 24 * i
                if i == 1:
                    ml_roots(0)
                splits(c, 5, 7)
                if i == 0:
                    fox_copies(3)
                else:
                    ml_out_hi(0)
                splits(c, 7, 11)
                if i == 0:
                    fox_out_hi(3)
                ml_exps(i, 0)
                splits(c, 11, 15)
                ml_exps(i, 1)
                splits(c, 15, 16)
                ml_copies(i, 0)
                splits(c, 16, 20)
                ml_copies(i, 1)
                splits(c, 20, 23)
                for m in range(2):
                    if m == 1:
                        splits(c, 23, 27)
                    act.wait_ge(scaled, Z_ML + 6 * i + 5 + m)
                    nc.scalar.activation(MO[:, m, :, :], MO[:, m, :, :], ACT.Sigmoid).then_inc(m_gate, 1)
                    act.wait_ge(m_hm, 2 * i + m + 1)
                    nc.scalar.activation(SQ[:, m, :, :], HM[:, m, :, :], ACT.Square).then_inc(m_sq, 1)
                splits(c, 27, 29)

            def merge(i, first):
                c = C_MG + i * 12
                if first:
                    ml_roots(1)
                splits(c, 5, 7)
                if first:
                    ml_out_hi(1)
                for n in range(2):
                    act.wait_ge(scaled, i * 2 + (Z_MG + n + 1))
                    nc.scalar.activation(SG[:, n, :, :], SG[:, n, :, :], ACT.Sigmoid).then_inc(sg_ready, 1)
                    splits(c, *((7, 11), (11, 15))[n])
                splits(c, 15, 16)
                act.wait_ge(merged_ready, i + 1)
                nc.scalar.activation(MHL[:, bass.ds(i * 2, 2), 0:S], T1[:, :, :], ACT.Copy).then_inc(mhi_ready, 1)
                splits(c, 16, 17)

            merge(0, True)
            with act.Fori(0, 7) as i:
                merge(i + 1, False)

            def square(c0, kts, n, name):
                per = len(kts)

                def body(i, final=False):
                    c = c0 + i * (2 * per)
                    for h in range(2):
                        end = (h + 1) * per
                        stop = end + (0 if final and h else 5)
                        splits(c, 5 + h * per, min(end + 4, stop), kts + kts)
                        act.wait_ge(x_added, i * 2 + (8 * (n - 1) + h + 1))
                        nc.scalar.activation(YC[:, 2:4, :], X[:, bass.ds(i * 4 + 2 * h, 2), :], ACT.Square
                                             ).then_inc(x_squared, 1)
                        if name is not None:
                            for k in range(2):
                                gain_hi(name, i * 4 + (2 * h + k), i * 4 + (2 * h + k))
                        splits(c, min(end + 4, stop), stop, kts + kts)

                last = name is None
                with act.Fori(0, 3 if last else 4) as i:
                    body(i)
                if last:
                    body(3, True)

            def up(c0, z0, ff, it0, n, cw, cb, func):
                tiles = ff // P

                def tap(z, side, col):
                    act.wait_ge(scaled, z)
                    for m in range(2):
                        nc.scalar.activation(YC[:, 2 * side + m, :], UP[:, side, m, 2:S + 2], ACT.Identity,
                                             scale=VEC[:, bass.ds(col + (COL[cw] + 2 * 2 * tiles + m), 1)],
                                             bias=VEC[:, bass.ds(col + (COL[cb] + m), 1)]).then_inc(tap_ready, 1)

                def body(i, first):
                    c, z = c0 + i * 8, z0 + i * 2
                    if first:
                        norm_root_of(n)
                    splits(c, 5, 8)
                    tap(z + 1, 0, i * 2)
                    splits(c, 8, 11)
                    act.wait_ge(conv_ready, i * 8 + (8 * it0 + 4))
                    nc.scalar.activation(YC[:, 0:2, :], YC[:, 0:2, :], func).then_inc(gate_act, 1)
                    splits(c, 11, 12)
                    tap(z + 2, 1, i * 2 + tiles)
                    splits(c, 12, 13)
                    act.wait_ge(hid_ready, i + (it0 + 1))
                    nc.scalar.activation(H[:, bass.ds(i * 2, 2), 0:S], YC[:, 0:2, :], ACT.Copy).then_inc(hhi_ready, 1)

                body(0, True)
                with act.Fori(1, ff // GROUP) as i:
                    body(i, False)

            square(C_OUT, [4] * 4, 1, "norm2_g")
            up(C_UP, Z_UP, FF1, 0, 1, "conv_w", "conv_b", ACT.Silu)
            square(C_DN, KT1, 2, "norm1_g_2")

            act.wait_ge(c8_abs, 1)
            nc.scalar.activation(RI[:, 0, 0:8], RI[:, 0, 8:16], ACT.Exp, scale=-1.0).then_inc(c8_exp, 1)
            act.wait_ge(c8_exp, 1)
            nc.scalar.activation(RI[:, 0, 0:8], RI[:, 0, 0:8], ACT.Ln, bias=ONES[:, 0:1]).then_inc(c8_ln, 1)
            norm_root_of(2)
            splits(C_XL, 5, 20)

            def gelu(g, count, dst, first):
                act.wait_ge(scaled, g)
                nc.scalar.activation(dst, ZT[:, :, :], ACT.Gelu_apprx_tanh).then_inc(gelu_done, 1)

            act.sem_inc(gelu_done, 1)
            with act.Fori(0, 4) as i:
                for n in range(2):
                    c, g, k = C_ZU + i * 8, i * 2 + (Z_ZU + n), i * 2 + n
                    splits(c, 4 + 5 * n, 6 + 4 * n)
                    act.wait_ge(lru_done, k + 1)
                    act.wait_ge(c8_ready, 1)
                    nc.scalar.activation(XR[:, :], XL[:, bass.ds(k, 1), 3:S + 3], ACT.Identity,
                                         scale=VEC[:, bass.ds(k + (COL["lru_conv_w_2"] + 24), 1)],
                                         bias=VEC[:, bass.ds(k + COL["lru_conv_b_2"], 1)]).then_inc(xr_tap, 1)
                    splits(c, 6 + 4 * n, 7 + 4 * n)
                    gelu(g + 1, None, GZ[:, bass.ds(k * 2, 2), :], None)
                    act.wait_ge(lru_acc, k + (1 + 2))
                    for a, bias in enumerate(("lru_ba_2", "lru_bx_2")):
                        nc.scalar.activation(RI[:, a, :], PS[:, 4, a * S:a * S + S], ACT.Sigmoid,
                                             bias=VEC[:, bass.ds(k + COL[bias], 1)]).then_inc(lru_gates, 1)
                    act.wait_ge(lru_gates, k * 2 + (1 + 2))
                    nc.scalar.activation(LA[:, :], RI[:, 0, :], ACT.Exp, scale=C8[:, bass.ds(k, 1)]).then_inc(lru_th, 1)
                    nc.scalar.activation(LT[:, :], RI[:, 0, :], ACT.Tanh, scale=C8[:, bass.ds(k, 1)]).then_inc(lru_th, 1)
                    act.wait_ge(lru_q, k + 1)
                    nc.scalar.activation(LM[:, :], LM[:, :], ACT.Sqrt, scale=-1.0).then_inc(lru_mult, 1)
                    splits(c, 7 + 4 * n, 9 + 3 * n)

            act.wait_ge(ln_centered, 1)
            nc.scalar.activation(SQV[:, :, :], GZ[:, 8:16, :], ACT.Square).then_inc(ln_sq, 1)
            act.wait_ge(ln_acc, 2)
            nc.scalar.activation(LT[:, :], PS[:, 5, S:2 * S], ACT.Sqrt, bias=EPS5[:, :], scale=1.0 / 1024
                                 ).then_inc(ln_root, 1)
            act.wait_ge(ln_ready, 1)
            with act.Fori(0, 2) as i:
                for n in range(2):
                    c, g, k = C_GL + i * 8, i * 2 + (Z_GL + n), i * 2 + n
                    splits(c, 4 + 5 * n, 6 + 4 * n)
                    act.wait_ge(vtk_acc, k + 1)
                    for m in range(2):
                        nc.scalar.activation(VNS[:, m, :], GZ[:, bass.ds(k * 2 + (8 + m), 1), :], ACT.Identity,
                                             scale=VEC[:, bass.ds(k * 2 + (COL["gm_v_g_2"] + m), 1)],
                                             bias=VEC[:, bass.ds(k * 2 + (COL["gm_v_b_2"] + m), 1)]
                                             ).then_inc(vn_ready, 1)
                    act.wait_ge(vtk_acc, k + 2)
                    nc.scalar.activation(VTK[:, :, :, :].rearrange("p m b d -> p (m b d)"), PS[:, 6, :], ACT.Copy
                                         ).then_inc(vtk_ready, 1)
                    splits(c, 6 + 4 * n, 7 + 4 * n)
                    gelu(g + 1, None, GL[:, bass.ds(k * 2, 2), :], None)
                    splits(c, 7 + 4 * n, 9 + 3 * n)

            act.wait_ge(mixed_ready, 4 + 1)
            nc.scalar.activation(SQV[:, :, :], GZ[:, 0:8, :], ACT.Square).then_inc(f_sq, 1)
            act.wait_ge(f_in, 1)
            nc.scalar.activation(GZ[:, 8:16, :], HL[:, :, :], ACT.Square).then_inc(f_sq, 1)
            for n, dst in enumerate((RSTD, MU)):
                act.wait_ge(f_acc, n + 1)
                nc.scalar.activation(dst[:, :], PS[:, 4 + n, 0:S], ACT.Sqrt, bias=EPS1[:, :], scale=1.0 / 1024
                                     ).then_inc(f_root, 1)
            for n, (src, name) in enumerate(((GZ, "gm_out_g_2"), (HL, "lru_out_g_2"))):
                act.wait_ge(f_scaled, n + 1)
                for k in range(8):
                    nc.scalar.activation(AHL[:, 8 * n + k, 0:S], src[:, k, :], ACT.Copy,
                                         scale=VEC[:, COL[name] + k:COL[name] + k + 1]).then_inc(f_hi, 1)

            splits(C_O2, 4, 5)
            square(C_O2, [4] * 4, 3, "norm2_g_2")
            up(C_U2, Z_U2, FF2, 22, 3, "ffn_conv_w_2", "ffn_conv_b_2", ACT.Gelu_apprx_tanh)
            square(C_D2, KT2, 4, None)
            norm_root_of(4)

        @block.vector
        def _(dve):
            own = Chain(dve, dve_own)

            def lo(c, j, kt=4):
                s = j % RING
                dve.wait_ge(hi_ready, c + (j + 1))
                nc.vector.tensor_tensor(LO[:, s, 0:kt, :], RAW[:, s, 0:kt, :], HI[:, s, 0:kt, :].bitcast(F32),
                                        ALU.subtract).then_inc(lo_ready, 1)

            def splits(c, a, b, kts=()):
                for j in range(a, b):
                    lo(c, j, kts[j] if j < len(kts) else 4)

            def evacuate(c, end, buf, out):
                dve.wait_ge(chunk_used, c + (end + RING))
                nc.vector.tensor_reduce(out, acc(buf), AX.X, ALU.add).then_inc(acc_evacuated, 1)

            def evacuated(g):
                dve.wait_ge(acc_evacuated, g + 2)

            def tt(out, a, b, op):
                return nc.vector.tensor_tensor(out, a, b, op)

            def stt(out, a, s, b, op0, op1, **kw):
                return nc.vector.scalar_tensor_tensor(out=out, in0=a, scalar=s, in1=b, op0=op0, op1=op1, **kw)

            def vec(name, k):
                return VEC[:, COL[name] + k:COL[name] + k + 1]

            def norm_rstd(n):
                dve.wait_ge(norm_root, n + 1)
                nc.vector.reciprocal(RSTD[:, :], RSTD[:, :]).then_inc(rstd_ready, 1)
                dve.wait_ge(rstd_ready, n + 1)

            def scale(g, out):
                dve.wait_ge(acc_evacuated, g + 2)
                tt(out, out, RSTD[:, :].unsqueeze(1).to_broadcast([P, 2, S]), ALU.mult).then_inc(scaled, 1)

            def gain_lo(name, n, k):
                dve.wait_ge(nhi_ready, k + (KD * n + 1))
                stt(YHL[:, at_tile(k), S:2 * S], X[:, at_tile(k), :], VEC[:, at_tile(k, COL[name])],
                    YHL[:, at_tile(k), 0:S].bitcast(F32), ALU.mult, ALU.subtract).then_inc(nlo_ready, 1)

            dve_start = nc.vector.memset(SQSUM[:, :, :], 0.0)
            own.mark(dve_start)
            dve.sem_inc(acc_evacuated, 2)

            dve.wait_ge(vec_landed, 16)
            for q in range(4):
                for k in range(4 * q, 4 * q + 4):
                    gain_lo("norm1_g", 0, k)
                if q < 3:
                    splits(C_FOX, q, q + 1)
                dve.wait_ge(x_squared, q + 1)
                nc.vector.tensor_reduce(SQQ[:, q, :], XSQ[:, 4 * q:4 * q + 4, :].rearrange("p k n -> p n k"),
                                        AX.X, ALU.add).then_inc(sq_summed, 1)
            own.mark(nc.vector.tensor_scalar(QG[:, :], vec("q_norm_g", 0), float(FOX_HD) ** -0.5, None, ALU.mult))
            dve.wait_ge(wg_hi, 1)
            tt(WGL[:, :, :], WG[:, :, :], WGH[:, :, :].bitcast(F32), ALU.subtract).then_inc(wg_lo, 1)
            splits(C_FOX, 3, 4)
            norm_rstd(0)
            splits(C_FOX, 4, 5)

            def gates():
                dve.wait_ge(rcol_ready, 1)
                dve.wait_ge(gates_acc, 1)
                dve.wait_ge(gate_b_landed, 16)
                own.mark(nc.vector.tensor_copy(RCOL[:, 0:2], PS[:, 6, 0:2]))
                own.settle()
                for tb in range(2):
                    own.mark(stt(GZT[:, tb, :], PS[:, 4 + tb, 0:16], RCOL[:, tb:tb + 1], GB[:, :], ALU.mult, ALU.add))
                own.settle()
                stt(GA_[:, :, :], GZT[:, :, :], -1.0, GZT[:, :, :], ALU.mult, ALU.max).then_inc(gate_abs, 1)
                own.mark(nc.vector.tensor_scalar(NLF[:, :, :], GZT[:, :, 0:NG], 0.0, None, ALU.min))
                own.mark(nc.vector.memset(GI[:, :, :], 0.0))
                own.settle()
                nc.vector.tensor_copy(GI[:, :, FOX_HEADS:NG], GZT[:, :, NG:16]).then_inc(logf_ready, 1)
                dve.wait_ge(gate_ln, 1)
                tt(LF[:, :, :], NLF[:, :, :], GE[:, :, 0:NG], ALU.subtract).then_inc(logf_ready, 1)
                dve.wait_ge(logf_ready, 2)
                nc.vector.tensor_scalar(NLF[:, :, :], LF[:, :, :], -1.0, None, ALU.mult).then_inc(logf_ready, 1)

            def cumulated():
                dve.wait_ge(cum_acc, 1)
                nc.vector.tensor_copy(CUM[:, :, :], PS[:, 6, 0:32].rearrange("p (b h) -> p h b", b=2)[:, 0:NG, :]
                                      ).then_inc(cum_ready, 1)
                nc.vector.tensor_copy(ROWS[:, :], PS[0:NG, 7, 0:S]).then_inc(cum_ready, 1)
                dve.wait_ge(cum_ready, 2)
                own.mark(nc.vector.tensor_scalar(NCUM[:, :, :], CUM[:, :, :], -1.0, None, ALU.mult))
                own.settle()

            def select_rows(h0):
                for m in range(2):
                    nc.vector.tensor_scalar(RSEL[:, m, :], ROWS[:, :], IDENT[0:NG, bass.ds(h0 + m, 1)], None,
                                            ALU.mult).then_inc(rsel_ready, 1)

            def fox_diagonals(i):
                dve.wait_ge(col_roots, i + 1)
                own.mark(nc.vector.reciprocal(RCOL[:, :], RCOL[:, :]))
                own.settle()
                tt(DG[:, :, :, :].rearrange("p a b d -> p (a b) d"), IDENT[:, :].unsqueeze(1).to_broadcast([P, 8, P]),
                   RCOL[:, :].unsqueeze(2).to_broadcast([P, 8, P]), ALU.mult).then_inc(dg_ready, 1)

            def fox_norm(i):
                dve.wait_ge(sums_ready, i + 1)
                dve.wait_ge(scaled, i * 3 + (Z_FOX + 2))
                dve.wait_ge(rsel_ready, i * 2 + 2)
                own.mark(stt(QT[:, :, :], QT[:, :, :], QG[:, :], PS[:, 6, :].rearrange("p (m n) -> p m n", m=2),
                             ALU.mult, ALU.mult))
                own.settle()
                stt(KTT[:, :, :], KTT[:, :, :], vec("k_norm_g", 0), PS[:, 7, :].rearrange("p (m n) -> p m n", m=2),
                    ALU.mult, ALU.mult).then_inc(qk_normed, 1)

            def masked(i, m, h, bank, cum):
                for b, cols in enumerate((slice(0, P), slice(P, 384))):
                    own.mark(stt(LG[:, m, cols], PS[:, bank, cols], cum[:, bass.ds(h, 1), b:b + 1], MASK[:, cols],
                                 ALU.add, ALU.add))
                own.settle()
                for b, cols in enumerate((slice(0, P), slice(P, 384))):
                    own.mark(nc.vector.tensor_reduce(MX[:, m, b:b + 1], LG[:, m, cols], AX.X, ALU.max))
                own.settle()

            def normalise(m, signal):
                own.mark(nc.vector.reciprocal(RS[:, m, :], RS[:, m, :]))
                own.settle()
                own.mark(nc.vector.tensor_scalar(LG[:, m, 0:P], LG[:, m, 0:P], RS[:, m, 0:1], None, ALU.mult))
                own.settle()
                nc.vector.tensor_scalar(LG[:, m, P:384], LG[:, m, P:384], RS[:, m, 1:2], None, ALU.mult
                                        ).then_inc(signal, 1)

            def fox_maxima(i):
                for m in range(2):
                    dve.wait_ge(logits_ready, i * 2 + (m + 1))
                    masked(i, m, i * 2 + m, 4 + m, CUM)
                    nc.vector.tensor_scalar(NM[:, m, :], MX[:, m, :], -1.0, None, ALU.mult).then_inc(negmax_ready, 1)

            def fox_probabilities(i):
                for m in range(2):
                    dve.wait_ge(exp_ready, i * 4 + 2 * (m + 1))
                    normalise(m, prob_ready)

            def fox_out_lo(i):
                dve.wait_ge(ahi_ready, i + 1)
                tt(AHL[:, bass.ds(i * 2, 2), S:2 * S], PS[:, 7, :].rearrange("p (m n) -> p m n", m=2),
                   AHL[:, bass.ds(i * 2, 2), 0:S].bitcast(F32), ALU.subtract).then_inc(alo_ready, 1)

            def fox(i, first):
                c, z = C_FOX + i * 12, i * 3 + G_FOX
                splits(c, 5, 7)
                evacuate(c, 4, 0, QT[:, :, :])
                scale(z + 1, QT[:, :, :])
                splits(c, 7, 11)
                evacuate(c, 8, 1, KTT[:, :, :])
                scale(z + 2, KTT[:, :, :])
                if first:
                    dve.wait_ge(ident_made, 4)
                    gates()
                    cumulated()
                else:
                    fox_out_lo(i - 1)
                splits(c, 11, 12)
                select_rows(i * 2)
                fox_diagonals(i)
                splits(c, 12, 13)
                fox_norm(i)
                splits(c, 13, 15)
                evacuate(c, 12, 0, VT[:, 0, :, :])
                scale(z + 3, VT[:, 0, :, :])
                fox_maxima(i)
                splits(c, 15, 16)
                fox_probabilities(i)
                splits(c, 16, 17)

            fox(0, True)
            with dve.Fori(0, 3) as i:
                own.enter(i, 14)
                fox(i + 1, False)
                own.leave(3)

            def ml_weights(i, m):
                h = FOX_HEADS + 2 * i + m
                dve.wait_ge(m_rows, 2 * i + m + 1)
                masked(i, m, h, 4 + m, CUM)
                stt(NM[:, m, :], MX[:, m, :], -1.0, NCUM[:, h, :], ALU.mult, ALU.min).then_inc(m_negmax, 1)
                dve.wait_ge(m_qk, 2 * i + m + 1)
                dve.wait_ge(m_exp, 3 * (2 * i + m + 1))
                for b, cols in enumerate((slice(0, P), slice(P, 384))):
                    own.mark(stt(LG[:, m, cols], PS[:, 6 + m, cols], float(ML_DQK) ** -0.5, LG[:, m, cols],
                                 ALU.mult, ALU.mult, accum_out=RS[:, m, b:b + 1]))
                own.settle()
                own.mark(tt(EM[:, m, :], RS[:, m, :], EM[:, m, :], ALU.max))
                own.settle()
                own.mark(stt(RS[:, m, :], RS[:, m, :], -1.0, EM[:, m, :], ALU.mult, ALU.max))
                own.settle()
                normalise(m, m_prob)

            def ml_out(i):
                dve.wait_ge(m_rt, 2 * i + 2)
                own.mark(nc.vector.reciprocal(RT[:, :, 0, :], RT[:, :, 0, :]))
                dve.wait_ge(m_gate, 2 * i + 2)
                own.settle()
                for m in range(2):
                    for t in range(2):
                        own.mark(stt(HM[:, m, t, :], HM[:, m, t, :], vec("m_norm_g", 4 * i + 2 * m + t),
                                     RT[:, m, 0, :], ALU.mult, ALU.mult))
                own.settle()
                for m in range(2):
                    tt(HM[:, m, :, :], HM[:, m, :, :], MO[:, m, :, :], ALU.mult).then_inc(m_out, 1)
                for m in range(2):
                    dve.wait_ge(m_ahi, 2 * i + m + 1)
                    ks = slice(8 + 4 * i + 2 * m, 10 + 4 * i + 2 * m)
                    tt(AHL[:, ks, S:2 * S], HM[:, m, :, :], AHL[:, ks, 0:S].bitcast(F32), ALU.subtract
                       ).then_inc(m_alo, 1)

            for i in range(2):
                c, g = C_ML + 24 * i, G_ML + 6 * i
                splits(c, 5, 7)
                evacuate(c, 4, 1, QT[:, :, :])
                scale(g + 1, QT[:, :, :])
                if i == 1:
                    ml_out(0)
                select_rows(FOX_HEADS + 2 * i)
                splits(c, 7, 11)
                if i == 0:
                    fox_out_lo(3)
                evacuate(c, 8, 0, KTT[:, :, :])
                scale(g + 2, KTT[:, :, :])
                ml_weights(i, 0)
                splits(c, 11, 15)
                evacuate(c, 12, 1, VT[:, 0, :, :])
                scale(g + 3, VT[:, 0, :, :])
                ml_weights(i, 1)
                splits(c, 15, 19)
                evacuate(c, 16, 0, VT[:, 1, :, :])
                scale(g + 4, VT[:, 1, :, :])
                splits(c, 19, 23)
                for m in range(2):
                    if m == 1:
                        splits(c, 23, 27)
                    evacuate(c, 20 + 4 * m, 1 - m, MO[:, m, :, :])
                    scale(g + 5 + m, MO[:, m, :, :])
                    dve.wait_ge(m_pv, 2 * i + m + 1)
                    nc.vector.tensor_copy(HM[:, m, :, :], PS[:, 4 + m, :].rearrange("p (t n) -> p t n", t=2)
                                          ).then_inc(m_hm, 1)
                splits(c, 27, 29)

            def merge(i, first):
                c, g = C_MG + i * 12, G_MG + i * 4
                splits(c, 5, 7)
                if not first:
                    dve.wait_ge(mhi_ready, i)
                evacuate(c, 4, 1, SG[:, 0, :, :])
                scale(g + 1, SG[:, 0, :, :])
                if first:
                    ml_out(1)
                splits(c, 7, 11)
                evacuate(c, 8, 0, SG[:, 1, :, :])
                scale(g + 2, SG[:, 1, :, :])
                splits(c, 11, 13)
                evacuate(c, 10, 1, T1[:, :, :])
                splits(c, 13, 15)
                evacuate(c, 12, 0, T2[:, :, :])
                splits(c, 15, 16)
                dve.wait_ge(sg_ready, i * 2 + 2)
                evacuated(g + 4)
                own.mark(tt(T1[:, :, :], T1[:, :, :], SG[:, 0, :, :], ALU.mult))
                own.mark(tt(T2[:, :, :], T2[:, :, :], SG[:, 1, :, :], ALU.mult))
                own.settle()
                tt(T1[:, :, :], T1[:, :, :], T2[:, :, :], ALU.add).then_inc(merged_ready, 1)
                dve.wait_ge(mhi_ready, i + 1)
                tt(MHL[:, bass.ds(i * 2, 2), S:2 * S], T1[:, :, :], MHL[:, bass.ds(i * 2, 2), 0:S].bitcast(F32),
                   ALU.subtract).then_inc(mlo_ready, 1)
                splits(c, 16, 17)

            merge(0, True)
            with dve.Fori(0, 7) as i:
                own.enter(i, 2)
                merge(i + 1, False)
                own.leave(7)

            def square(c0, g0, kts, n, name):
                per = len(kts)
                own.mark(nc.vector.memset(SQSUM[:, :, :], 0.0))
                own.settle()

                def body(i, final=False):
                    c = c0 + i * (2 * per)
                    for h in range(2):
                        end = (h + 1) * per
                        stop = end + (0 if final and h else 5)
                        splits(c, 5 + h * per, min(end + 3, stop), kts + kts)
                        evacuate(c, end, 1 - h, YC[:, 0:2, :])
                        evacuated(g0 + i * 2 + (h + 1))
                        xs = X[:, bass.ds(i * 4 + 2 * h, 2), :]
                        tt(xs, xs, YC[:, 0:2, :], ALU.add).then_inc(x_added, 1)
                        splits(c, min(end + 3, stop), min(end + 4, stop), kts + kts)
                        dve.wait_ge(x_squared, i * 2 + (4 + 8 * (n - 1) + h + 1))
                        dve.wait_ge(x_added, i * 2 + (8 * (n - 1) + h + 1))
                        tt(SQSUM[:, :, :], SQSUM[:, :, :], YC[:, 2:4, :], ALU.add).then_inc(sq_added, 1)
                        if name is not None:
                            for k in range(2):
                                gain_lo(name, n, i * 4 + (2 * h + k))
                        splits(c, min(end + 4, stop), stop, kts + kts)
                        dve.wait_ge(sq_added, i * 2 + (8 * (n - 1) + h + 1))

                last = name is None
                with dve.Fori(0, 3 if last else 4) as i:
                    body(i)
                if last:
                    body(3, True)

            def up(c0, g0, z0, ff, it0, n, cw):
                tiles = ff // P
                own.mark(nc.vector.memset(UP[:, :, :, 0:2], 0.0))
                own.settle()

                def taps(i, side, col, z):
                    dve.wait_ge(scaled, z)
                    for tap in (1, 0):
                        for m in range(2):
                            if tap == 1:
                                dve.wait_ge(tap_ready, i * 4 + (4 * it0 + 2 * side + m + 1))
                            else:
                                dve.wait_ge(conv_ready, i * 8 + (8 * it0 + 4 * side + m + 1))
                            stt(YC[:, 2 * side + m, :], UP[:, side, m, tap:tap + S],
                                VEC[:, bass.ds(col + (COL[cw] + 2 * tap * tiles + m), 1)], YC[:, 2 * side + m, :],
                                ALU.mult, ALU.add).then_inc(conv_ready, 1)

                def body(i, first):
                    c, g, z = c0 + i * 8, g0 + i * 2, z0 + i * 2
                    if first:
                        norm_rstd(n)
                    splits(c, 5, 7)
                    evacuate(c, 4, 1, UP[:, 0, :, 2:S + 2])
                    scale(g + 1, UP[:, 0, :, 2:S + 2])
                    splits(c, 7, 8)
                    taps(i, 0, i * 2, z + 1)
                    splits(c, 8, 11)
                    evacuate(c, 8, 0, UP[:, 1, :, 2:S + 2])
                    scale(g + 2, UP[:, 1, :, 2:S + 2])
                    splits(c, 11, 12)
                    taps(i, 1, i * 2 + tiles, z + 2)
                    dve.wait_ge(gate_act, i + (it0 + 1))
                    dve.wait_ge(conv_ready, i * 8 + (8 * it0 + 8))
                    tt(YC[:, 0:2, :], YC[:, 0:2, :], YC[:, 2:4, :], ALU.mult).then_inc(hid_ready, 1)
                    splits(c, 12, 13)
                    dve.wait_ge(hhi_ready, i + (it0 + 1))
                    tt(H[:, bass.ds(i * 2, 2), S:2 * S], YC[:, 0:2, :], H[:, bass.ds(i * 2, 2), 0:S].bitcast(F32),
                       ALU.subtract).then_inc(hlo_ready, 1)

                body(0, True)
                with dve.Fori(1, ff // GROUP) as i:
                    body(i, False)

            K4 = [4] * 4
            square(C_OUT, G_OUT, K4, 1, "norm2_g")
            up(C_UP, G_UP, Z_UP, FF1, 0, 1, "conv_w")
            square(C_DN, G_DN, KT1, 2, "norm1_g_2")

            lam = VEC[:, COL["lru_lambda_2"]:COL["lru_lambda_2"] + 8]
            stt(RI[:, 0, 8:16], lam, -1.0, lam, ALU.mult, ALU.max).then_inc(c8_abs, 1)
            own.mark(nc.vector.tensor_scalar(RI[:, 0, 16:24], lam, -1.0, 0.0, ALU.mult, ALU.max))
            own.mark(nc.vector.memset(XL[:, :, 0:3], 0.0))
            own.settle()
            dve.wait_ge(c8_ln, 1)
            own.mark(tt(RI[:, 0, 24:32], RI[:, 0, 16:24], RI[:, 0, 0:8], ALU.add))
            own.settle()
            nc.vector.tensor_scalar(C8[:, :], RI[:, 0, 24:32], -LRU_C, None, ALU.mult).then_inc(c8_ready, 1)

            norm_rstd(2)
            for n in range(4):
                splits(C_XL, 5 + 4 * n, 7 + 4 * n)
                evacuate(C_XL, 4 + 4 * n, 1 - n % 2, XL[:, 2 * n:2 * n + 2, 3:S + 3])
                scale(G_XL + n + 1, XL[:, 2 * n:2 * n + 2, 3:S + 3])
                splits(C_XL, 7 + 4 * n, 9 + 4 * n - (n == 3))

            dve.sem_inc(lru_done, 1)
            dve.wait_ge(scaled, Z_ZU)
            with dve.Fori(0, 4) as i:
                own.enter(i, 6)
                for n in range(2):
                    c, g, k = C_ZU + i * 8, G_ZU + i * 2 + n, i * 2 + n
                    splits(c, 4 + 5 * n, 6 + 4 * n)
                    for tap in (2, 1, 0):
                        if tap == 2:
                            dve.wait_ge(xr_tap, k + 1)
                        else:
                            dve.wait_ge(xr_ready, k * 3 + (2 - tap))
                        stt(XR[:, :], XL[:, bass.ds(k, 1), tap:tap + S],
                            VEC[:, bass.ds(k + (COL["lru_conv_w_2"] + 8 * tap), 1)], XR[:, :], ALU.mult, ALU.add
                            ).then_inc(xr_ready, 1)
                    splits(c, 6 + 4 * n, 7 + 4 * n)
                    dve.wait_ge(gelu_done, k + 1)
                    evacuate(c, 4 + 4 * n, 1 - n, ZT[:, :, :])
                    scale(g + 1, ZT[:, :, :])
                    dve.wait_ge(lru_th, k * 2 + 2)
                    own.mark(tt(LM[:, :], LA[:, :], LA[:, :], ALU.mult))
                    own.settle()
                    stt(LM[:, :], LM[:, :], 1.0, LT[:, :], ALU.add, ALU.mult).then_inc(lru_q, 1)
                    own.mark(tt(RI[:, 1, :], RI[:, 1, :], XR[:, :], ALU.mult))
                    own.settle()
                    dve.wait_ge(lru_mult, k + 1)
                    own.mark(tt(RI[:, 1, :], RI[:, 1, :], LM[:, :], ALU.mult))
                    own.settle()
                    nc.vector.tensor_tensor_scan(HL[:, bass.ds(k, 1), :].rearrange("p o n -> p (o n)"), LA[:, :],
                                                 RI[:, 1, :], 0.0, ALU.mult, ALU.add).then_inc(lru_done, 1)
                    splits(c, 7 + 4 * n, 9 + 3 * n)
                own.leave(4)

            def over_tiles(src):
                return src.rearrange("p k n -> p n k")

            def on_tiles(row):
                return row.unsqueeze(1).to_broadcast([P, 8, S])

            V = GZ[:, 8:16, :]
            dve.wait_ge(gelu_done, 8 + 1)
            nc.vector.tensor_reduce(SQSUM[:, 0, :], over_tiles(V), AX.X, ALU.add).then_inc(ln_sum, 1)
            dve.wait_ge(ln_acc, 1)
            own.mark(nc.vector.tensor_scalar(MU[:, :], PS[:, 5, 0:S], 1.0 / 1024, None, ALU.mult))
            own.settle()
            tt(V, V, on_tiles(MU[:, :]), ALU.subtract).then_inc(ln_centered, 1)
            dve.wait_ge(ln_sq, 1)
            nc.vector.tensor_reduce(SQSUM[:, 1, :], over_tiles(SQV[:, :, :]), AX.X, ALU.add).then_inc(ln_sum, 1)
            dve.wait_ge(ln_root, 1)
            own.mark(nc.vector.reciprocal(LT[:, :], LT[:, :]))
            own.settle()
            tt(V, V, on_tiles(LT[:, :]), ALU.mult).then_inc(ln_ready, 1)

            with dve.Fori(0, 2) as i:
                for n in range(2):
                    c, g, k = C_GL + i * 8, G_GL + i * 2 + n, i * 2 + n
                    splits(c, 4 + 5 * n, 7 + 4 * n)
                    dve.wait_ge(gelu_done, k + (8 + 1))
                    evacuate(c, 4 + 4 * n, 1 - n, ZT[:, :, :])
                    scale(g + 1, ZT[:, :, :])
                    dve.wait_ge(mix_acc, k + 1)
                    U = GZ[:, bass.ds(k * 2, 2), :]
                    tt(U, U, PS[:, 7, :].rearrange("p (m n) -> p m n", m=2), ALU.mult).then_inc(mixed_ready, 1)
                    splits(c, 7 + 4 * n, 9 + 3 * n)

            dve.wait_ge(gelu_done, 12 + 1)
            dve.wait_ge(lru_done, 8 + 1)
            tt(HL[:, :, :], HL[:, :, :], GL[:, :, :], ALU.mult).then_inc(f_in, 1)
            for n, src in enumerate((SQV[:, :, :], GZ[:, 8:16, :])):
                dve.wait_ge(f_sq, n + 1)
                nc.vector.tensor_reduce(SQSUM[:, n, :], over_tiles(src), AX.X, ALU.add).then_inc(f_sum, 1)
            dve.wait_ge(f_in, 1)
            for n, (row, src) in enumerate(((RSTD, GZ[:, 0:8, :]), (MU, HL[:, :, :]))):
                dve.wait_ge(f_root, n + 1)
                own.mark(nc.vector.reciprocal(row[:, :], row[:, :]))
                own.settle()
                tt(src, src, on_tiles(row[:, :]), ALU.mult).then_inc(f_scaled, 1)
            dve.wait_ge(f_scaled, 2)
            for n, (src, name) in enumerate(((GZ, "gm_out_g_2"), (HL, "lru_out_g_2"))):
                for k in range(8):
                    dve.wait_ge(f_hi, 8 * n + k + 1)
                    stt(AHL[:, 8 * n + k, S:2 * S], src[:, k, :], vec(name, k),
                        AHL[:, 8 * n + k, 0:S].bitcast(F32), ALU.mult, ALU.subtract).then_inc(f_lo, 1)

            splits(C_O2, 4, 5)
            square(C_O2, G_O2, K4, 3, "norm2_g_2")
            up(C_U2, G_U2, Z_U2, FF2, 22, 3, "ffn_conv_w_2")
            square(C_D2, G_D2, KT2, 4, None)
            norm_rstd(4)
            for k in range(KD):
                stt(X[:, k, :], X[:, k, :], vec("final_g_2", k), RSTD[:, :], ALU.mult, ALU.mult
                    ).then_inc(out_ready, 1)


_WEIGHTS = ["w_in", "w_proj_a", "w_proj_m", "w_out", "w_up", "w_down", "w_in_2", "w_out_2", "ffn_w_up_2",
            "ffn_w_down_2"]


def kernel(**inputs):
    import numpy as np
    import concourse.bacc as bacc
    from concourse.bass_utils import run_bass_kernel_spmd as run

    f = {n: np.asarray(a) for n, a in inputs.items()}
    arrays = {n: np.ascontiguousarray(f[n].reshape(f[n].shape[-2:])) for n in _WEIGHTS}
    arrays["x"] = np.ascontiguousarray(f["x"].reshape(S, KD, P).transpose(2, 1, 0))
    arrays["vec"] = np.ascontiguousarray(
        np.concatenate([f[name].reshape(tiles, P) for name, tiles in VECTORS]).T)
    w_in = arrays["w_in"]
    gate_columns = np.concatenate([w_in[:, OFF_FF:OFF_FF + FOX_HEADS], w_in[:, OFF_MF:OFF_MF + ML_HEADS],
                                   w_in[:, OFF_MI:OFF_MI + ML_HEADS]], axis=1)
    arrays["w_gate"] = np.ascontiguousarray(gate_columns.reshape(KD, P, 16).transpose(1, 0, 2))
    arrays["gate_b"] = np.concatenate([f["fox_f_bias"].reshape(1, -1), f["m_f_bias"].reshape(1, -1),
                                       f["m_i_bias"].reshape(1, -1)], axis=1)
    arrays["gm_ws_2"] = np.ascontiguousarray(f["gm_ws_2"][0].transpose(2, 0, 1))
    arrays["gm_bs_2"] = np.ascontiguousarray(f["gm_bs_2"].reshape(1, 8 * P))
    arrays["lru_wa_2"] = np.ascontiguousarray(f["lru_wa_2"][0].transpose(1, 0, 2))
    arrays["lru_wx_2"] = np.ascontiguousarray(f["lru_wx_2"][0].transpose(1, 0, 2))

    nc = bacc.Bacc("TRN2", target_bir_lowering=False, num_devices=1)
    w = {n: nc.dram_tensor(f"in_{n}", a.shape, F32, kind="ExternalInput").ap() for n, a in arrays.items()}
    w["out"] = nc.dram_tensor("out", (P, KD, S), F32, kind="ExternalOutput").ap()
    build(nc, w)
    r = run(nc, [{f"in_{n}": a for n, a in arrays.items()}], core_ids=[0])
    out = r.results[0]["out"]
    return np.ascontiguousarray(out.transpose(2, 1, 0)).reshape(1, S, D)
```

```python
from contextlib import ExitStack

import concourse.bass as bass
from concourse import mybir

F32 = mybir.dt.float32
F32R = mybir.dt.float32r
ALU = mybir.AluOpType
ACT = mybir.ActivationFunctionType
AX = mybir.AxisListType

P = 128
S = 256
D = 2048
KD = D // P
GROUP = 256
RING = 4
KT = 4
EPS = 1e-6
LN_EPS = 1e-5

FOX_HEADS, FOX_HD = 8, 128
ML_HEADS, ML_DQK, ML_DV = 4, 128, 256
NG = FOX_HEADS + ML_HEADS
OFF_FQ, OFF_FK, OFF_FV = 0, 1024, 2048
OFF_FF = 3072
OFF_MQ = OFF_FF + FOX_HEADS
OFF_MK = OFF_MQ + 512
OFF_MV = OFF_MK + 512
OFF_MO = OFF_MV + 1024
OFF_MI = OFF_MO + 1024
OFF_MF = OFF_MI + ML_HEADS
OFF_GA = OFF_MF + ML_HEADS
OFF_GM = OFF_GA + D
FF1, FF2 = 5632, 6144
KT1 = [4] * 8 + [3] * 4
KT2 = [4] * 12
LRU_C = 8.0

VECTORS = [("norm1_g", 16), ("q_norm_g", 1), ("k_norm_g", 1), ("m_norm_g", 8), ("norm2_g", 16),
           ("conv_w", 3 * 88), ("conv_b", 88), ("norm1_g_2", 16), ("gm_v_g_2", 8), ("gm_v_b_2", 8),
           ("lru_conv_w_2", 32), ("lru_conv_b_2", 8), ("lru_ba_2", 8), ("lru_bx_2", 8),
           ("lru_lambda_2", 8), ("gm_out_g_2", 8), ("lru_out_g_2", 8), ("norm2_g_2", 16),
           ("ffn_conv_w_2", 3 * 96), ("ffn_conv_b_2", 96), ("final_g_2", 16)]
COL, _n = {}, 0
for _name, _tiles in VECTORS:
    COL[_name] = _n
    _n += _tiles
NVEC = _n
NFIRST = COL["norm2_g"]


class Chain:

    def __init__(self, eng, sem):
        self.eng, self.sem, self.base, self.k, self.it, self.per = eng, sem, 0, 0, None, 0

    def mark(self, ins):
        ins.then_inc(self.sem, 1)
        self.k += 1

    def settle(self):
        n = self.base + self.k
        self.eng.wait_ge(self.sem, n if self.it is None else self.it * self.per + n)

    def enter(self, it, per):
        self.base, self.k, self.it, self.per = self.base + self.k, 0, it, per

    def leave(self, n):
        assert self.k == self.per, f"the loop's body marks {self.k}"
        self.base, self.k, self.it, self.per = self.base + n * self.per, 0, None, 0


def build(nc, w):
    stack = ExitStack()
    with stack:
        at = {}
        cursor = [16512]

        def here(name, shape, dt, offset=None):
            size = 4
            for n in shape[1:]:
                size *= n
            if offset is None:
                offset = cursor[0]
                cursor[0] += (size + 31) // 32 * 32
            at[name] = offset
            return nc.alloc_sbuf_tensor_at(name, shape, dt, offset=offset)

        X = here("X", [P, KD, S], F32)
        YHL = here("YHL", [P, KD, 2 * S], F32R)
        H = here("H", [P, 48, 2 * S], F32R)
        RAW = here("RAW", [P, RING, KT, GROUP], F32)
        HI = here("HI", [P, RING, KT, GROUP], F32R)
        LO = here("LO", [P, RING, KT, GROUP], F32R)
        VEC = here("VEC", [P, NVEC], F32)
        ONES = here("ONES", [P, P], F32)
        IDENT = here("IDENT", [P, P], F32)
        RSTD = here("RSTD", [P, S], F32)
        SQSUM = here("SQSUM", [P, 2, S], F32)
        QG = here("QG", [P, 1], F32)
        EPS1 = here("EPS1", [P, 1], F32)
        EPS5 = here("EPS5", [P, 1], F32)
        C8 = here("C8", [P, 8], F32)
        RCOL = here("RCOL", [P, 8], F32)
        WORK = cursor[0]
        assert WORK + 8224 <= 229368, WORK

        UP = here("UP", [P, 2, 2, S + 2], F32, WORK)
        YC = here("YC", [P, 4, S], F32, WORK + 4128)
        LG = here("LG", [P, 2, 384], F32, WORK)
        PTS = here("PTS", [P, 2, 384], F32, WORK + 3072)
        MASK = here("MASK", [P, 384], F32, WORK + 6144)
        CUM = here("CUM", [P, NG, 2], F32, WORK + 7680)
        NCUM = here("NCUM", [P, NG, 2], F32, WORK + 7776)
        MX = here("MX", [P, 2, 2], F32, WORK + 7872)
        NM = here("NM", [P, 2, 2], F32, WORK + 7904)
        RS = here("RS", [P, 2, 2], F32, WORK + 7936)
        EM = here("EM", [P, 2, 2], F32, WORK + 7968)
        SG = here("SG", [P, 2, 2, S], F32, WORK)
        T1 = here("T1", [P, 2, S], F32, WORK + 4096)
        T2 = here("T2", [P, 2, S], F32, WORK + 6144)
        ZT = here("ZT", [P, 2, S], F32, WORK)
        ST = here("ST", [P, 2, S], F32, WORK + 2048)
        BSR = here("BSR", [1, 8 * P], F32, WORK + 4096)

        AHL = H[:, 0:16]
        MHL = H[:, 16:32]
        M1 = at["H"] + 32 * 2048
        QT = here("QT", [P, 2, S], F32, M1)
        KTT = here("KTT", [P, 2, S], F32, M1 + 2048)
        VT = here("VT", [P, 2, 2, S], F32, M1 + 4096)
        SQ = here("SQ", [P, 2, 2, S], F32, M1 + 8192)
        RT = here("RT", [P, 2, 2, S], F32, M1 + 12288)
        DG = here("DG", [P, 4, 2, P], F32, M1 + 12288)
        VTOK = here("VTOK", [P, 2, 2, 256], F32, M1 + 16384)
        MO = here("MO", [P, 2, 2, S], F32, M1 + 20480)
        HM = here("HM", [P, 2, 2, S], F32, M1 + 24576)
        ROWS = here("ROWS", [NG, S], F32, M1 + 28672)
        RSEL = here("RSEL", [NG, 2, S], F32, M1 + 29696)
        TRI = here("TRI", [P, S], F32, M1 + 31744)
        XSQ = here("XSQ", [P, KD, S], F32, M1)
        WG = here("WG", [P, KD, 16], F32, M1 + 20480)
        WGH = here("WGH", [P, KD, 16], F32R, M1 + 21504)
        WGL = here("WGL", [P, KD, 16], F32R, M1 + 22528)
        GB = here("GB", [16, 1], F32, M1 + 23552)
        GZR = here("GZR", [16, S], F32, WORK)
        GZT = here("GZT", [P, 2, 16], F32, M1 + 24576)
        GA_ = here("GA_", [P, 2, 16], F32, M1 + 24704)
        GE = here("GE", [P, 2, 16], F32, M1 + 24832)
        LF = here("LF", [P, 2, NG], F32, M1 + 24960)
        NLF = here("NLF", [P, 2, NG], F32, M1 + 25088)
        GI = here("GI", [P, 2, NG], F32, M1 + 25216)
        SQQ = here("SQQ", [P, 4, S], F32, M1 + 25600)
        assert at["TRI"] + 1024 <= at["RAW"]

        M2 = at["H"] + 16 * 2048
        GZ = here("GZ", [P, 8, S], F32, M2)
        VTB = here("VTB", [P, 2, 8, P], F32, M2 + 8192)
        SQG = here("SQG", [P, 8, S], F32, M2 + 8192)
        XL = here("XL", [P, 8, S + 3], F32, M2 + 16384)
        AA = here("AA", [P, 8, S], F32, M2 + 16384)
        HL = here("HL", [P, 8, S], F32, M2 + 24704)
        QQ = here("QQ", [P, 8, S], F32, M2 + 32896)
        GL = here("GL", [P, 8, S], F32, M2 + 41088)
        RI = here("RI", [P, 2, 2, S], F32, M2 + 41088)
        LT = here("LT", [P, 2, S], F32, M2 + 45184)
        LA2 = here("LA2", [P, 2, S], F32, M2 + 47232)
        VGB = here("VGB", [P, 2, 8 * P], F32, M2 + 49280)
        SQL = here("SQL", [P, 8, S], F32, M2 + 49280)
        WST = here("WST", [P, 8, P], F32, M2 + 57472)
        WAX = here("WAX", [P, 2, 2, P], F32, M2 + 61568)
        MU = here("MU", [P, S], F32, M2 + 63616)
        VSUM = here("VSUM", [P, 2, 4], F32, M2 + 64640)
        NMEAN = here("NMEAN", [P, 2], F32, M2 + 64672)
        VSQ = here("VSQ", [P, 2], F32, M2 + 64704)
        HB = here("HB", [P, 16], F32, M2 + 64736)
        C8H = here("C8H", [P, 8], F32, M2 + 64800)
        C8W = here("C8W", [P, 3, 8], F32, M2 + 64832)
        assert M2 + 64928 <= at["RAW"]

        PS = stack.enter_context(nc.psum_tensor("PS", [P, 8, 512], F32))

        def acc(buf):
            return PS[:, 2 * buf:2 * buf + 2, :].rearrange("p m (h n) -> p m n h", h=2)

        def sem(name):
            return stack.enter_context(nc.semaphore(name))

        raw_landed = [sem(f"raw_landed{i}") for i in range(RING)]
        hi_ready, lo_ready = sem("hi_ready"), sem("lo_ready")
        chunk_used = sem("chunk_used")
        acc_evacuated = sem("acc_evacuated")
        x_landed = [sem(f"x_landed{i}") for i in range(4)]
        vec_landed, gate_w_landed, gate_b_landed = sem("vec_landed"), sem("gate_w_landed"), sem("gate_b_landed")
        vec_rest_landed = sem("vec_rest_landed")
        consts_made, ident_made = sem("consts_made"), sem("ident_made")
        x_squared, sq_summed, norm_acc, norm_root = sem("x_squared"), sem("sq_summed"), sem("norm_acc"), sem("norm_root")
        x_added, nhi_ready, nlo_ready, scaled = sem("x_added"), sem("nhi_ready"), sem("nlo_ready"), sem("scaled")
        rstd_ready, sq_added = sem("rstd_ready"), sem("sq_added")
        gates_ready, gates_turned, dg_ready = sem("gates_ready"), sem("gates_turned"), sem("dg_ready")
        col_sums, col_roots = sem("col_sums"), sem("col_roots")
        dve_own, pool_own = sem("dve_own"), sem("pool_own")
        wg_hi, wg_lo, gates_acc, gate_abs, gate_exp, gate_ln, logf_ready = [
            sem(n) for n in ("wg_hi", "wg_lo", "gates_acc", "gate_abs", "gate_exp", "gate_ln", "logf_ready")]
        rsel_ready = sem("rsel_ready")
        cum_acc, cum_ready = sem("cum_acc"), sem("cum_ready")
        sq_ready, sums_ready, qk_normed = sem("sq_ready"), sem("sums_ready"), sem("qk_normed")
        logits_ready, negmax_ready, exp_ready, prob_ready = [
            sem(n) for n in ("logits_ready", "negmax_ready", "exp_ready", "prob_ready")]
        vtr_ready, vtok_ready, ptr_ready, pts_ready = [
            sem(n) for n in ("vtr_ready", "vtok_ready", "ptr_ready", "pts_ready")]
        pv_ready, ahi_ready, alo_ready = sem("pv_ready"), sem("ahi_ready"), sem("alo_ready")
        m_rows, m_qk, m_negmax, m_exp, m_prob = [
            sem(n) for n in ("m_rows", "m_qk", "m_negmax", "m_exp", "m_prob")]
        m_vtr, m_vtok, m_ptr, m_pts, m_pv, m_hm, m_gate, m_sq, m_sums, m_rt, m_out, m_ahi, m_alo = [
            sem(n) for n in ("m_vtr", "m_vtok", "m_ptr", "m_pts", "m_pv", "m_hm", "m_gate", "m_sq", "m_sums",
                             "m_rt", "m_out", "m_ahi", "m_alo")]
        sg_ready, merged_ready, mhi_ready, mlo_ready = [
            sem(n) for n in ("sg_ready", "merged_ready", "mhi_ready", "mlo_ready")]
        tap_ready, conv_ready, gate_act, hid_ready, hhi_ready, hlo_ready = [
            sem(n) for n in ("tap_ready", "conv_ready", "gate_act", "hid_ready", "hhi_ready", "hlo_ready")]
        c8_exp, c8_ln, c8_ready, c8_abs = sem("c8_exp"), sem("c8_ln"), sem("c8_ready"), sem("c8_abs")
        xr_tap, xr_ready, wax_landed, lru_acc, lru_gates, lru_th, lru_q, lru_clamped, lru_mult, lru_in, lru_done = [
            sem(n) for n in ("xr_tap", "xr_ready", "wax_landed", "lru_acc", "lru_gates", "lru_th", "lru_q",
                             "lru_clamped", "lru_mult", "lru_in", "lru_done")]
        v_gelu, u_gelu, g_gelu, ws_landed, ws_masked, bs_landed, vgb_landed = [
            sem(n) for n in ("v_gelu", "u_gelu", "g_gelu", "ws_landed", "ws_masked", "bs_landed", "vgb_landed")]
        v_turned, v_tokens, ln_mean, ln_sq, ln_root, vn_ready, mix_acc, mixed_ready = [
            sem(n) for n in ("v_turned", "v_tokens", "ln_mean", "ln_sq", "ln_root", "vn_ready", "mix_acc",
                             "mixed_ready")]
        gm_sq, gm_acc, gm_root, lru_gated, lru_sq, lru_sums_acc, lru_root, out_gained, out_hi_ready, out_lo_ready = [
            sem(n) for n in ("gm_sq", "gm_acc", "gm_root", "lru_gated", "lru_sq", "lru_sums_acc", "lru_root",
                             "out_gained", "out_hi_ready", "out_lo_ready")]
        xg_ready, out_ready, out_done = sem("xg_ready"), sem("out_ready"), sem("out_done")

        C_FOX, G_FOX = 0, 0
        C_ML, G_ML = C_FOX + 48, G_FOX + 12
        C_MG, G_MG = C_ML + 48, G_ML + 12
        C_OUT, G_OUT = C_MG + 96, G_MG + 32
        C_UP, G_UP = C_OUT + 32, G_OUT + 8
        C_DN, G_DN = C_UP + 8 * 22, G_UP + 2 * 22
        C_XL, G_XL = C_DN + 96, G_DN + 8
        C_V, G_V = C_XL + 16, G_XL + 4
        C_U, G_U = C_V + 16, G_V + 4
        C_GL, G_GL = C_U + 16, G_U + 4
        C_O2, G_O2 = C_GL + 16, G_GL + 4
        C_U2, G_U2 = C_O2 + 32, G_O2 + 8
        C_D2, G_D2 = C_U2 + 8 * 24, G_U2 + 2 * 24

        Z_FOX, Z_ML, Z_MG, Z_UP = 0, 12, 24, 40
        Z_XL = Z_UP + 2 * 22
        Z_V, Z_U, Z_GL, Z_U2 = Z_XL + 4, Z_XL + 8, Z_XL + 12, Z_XL + 16

        FOX_OFFS = [OFF_FQ, OFF_FK, OFF_FV]

        def ml_cols(i):
            return [OFF_MQ + 256 * i, OFF_MK + 256 * i, OFF_MV + 512 * i, OFF_MV + 512 * i + 256,
                    OFF_MO + 512 * i, OFF_MO + 512 * i + 256]

        def at_tile(k, base=0):
            return bass.ds(k + base, 1)

        block = stack.enter_context(nc.Block())

        @block.sync
        def _(sp):
            def load(c, j, src, row, kts, col):
                sp.wait_ge(lo_ready, c + (j + 1))
                sp.dma_start(RAW[:, j % RING, 0:kts, :],
                             src[row:row + kts * P, bass.ds(col, GROUP)].rearrange("(k p) n -> p k n", p=P)
                             ).then_inc(raw_landed[j % RING], 16)

            def load_group(c, j, src, col, kts=(4, 4, 4, 4)):
                row = 0
                for n, k in enumerate(kts):
                    load(c, j + n, src, row, k, col)
                    row += k * P

            sp.sem_inc(lo_ready, RING)
            with sp.Fori(1, 5) as i:
                for n, off in enumerate(FOX_OFFS):
                    load_group(i * 12 + (C_FOX - 12), 4 * n, w["w_in"], i * 256 + (off - 256))
            for i in range(2):
                for n, off in enumerate(ml_cols(i)):
                    load_group(C_ML + 24 * i, 4 * n, w["w_in"], off)
            with sp.Fori(1, 9) as i:
                c = i * 12 + (C_MG - 12)
                load_group(c, 0, w["w_in"], i * 256 + (OFF_GA - 256))
                load_group(c, 4, w["w_in"], i * 256 + (OFF_GM - 256))
                load_group(c, 8, w["w_proj_a"], i * 256 - 256, (4, 4))
                load_group(c, 10, w["w_proj_m"], i * 256 - 256, (4, 4))

            def square(c, src, kts=(4, 4, 4, 4)):
                per = 2 * len(kts)
                with sp.Fori(1, 5) as i:
                    for n in range(2):
                        load_group(i * per + (c - per), n * len(kts), src, i * 512 + (n * 256 - 512), kts)

            def up(c, src, ff):
                with sp.Fori(1, ff // GROUP + 1) as i:
                    load_group(i * 8 + (c - 8), 0, src, i * 256 - 256)
                    load_group(i * 8 + (c - 8), 4, src, i * 256 + (ff - 256))

            square(C_OUT, w["w_out"])
            up(C_UP, w["w_up"], FF1)
            square(C_DN, w["w_down"], KT1)
            for c, off in ((C_XL, 3072), (C_V, 1024), (C_U, 0), (C_GL, 2048)):
                with sp.Fori(1, 3) as i:
                    for n in range(2):
                        load_group(i * 8 + (c - 8), 4 * n, w["w_in_2"], i * 512 + (off + 256 * n - 512))
            square(C_O2, w["w_out_2"])
            up(C_U2, w["ffn_w_up_2"], FF2)
            square(C_D2, w["ffn_w_down_2"], KT2)
            for q in range(4):
                sp.wait_ge(out_ready, q + 1)
                sp.dma_start(w["out"][:, 4 * q:4 * q + 4, :], X[:, 4 * q:4 * q + 4, :]).then_inc(out_done, 16)
            sp.wait_ge(out_done, 64)

        @block.gpsimd
        def _(pool):
            own = Chain(pool, pool_own)
            pool.dma_start(VEC[:, 0:NFIRST], w["vec"][:, 0:NFIRST]).then_inc(vec_landed, 16)
            for q in (2, 3):
                pool.dma_start(X[:, 4 * q:4 * q + 4, :], w["x"][:, 4 * q:4 * q + 4, :]).then_inc(x_landed[q], 16)
            pool.dma_start(WG[:, :, :], w["w_gate"]).then_inc(gate_w_landed, 16)
            pool.dma_start(GB[:, :], w["gate_b"]).then_inc(gate_b_landed, 16)
            pool.memset(ONES[:, :], 1.0).then_inc(consts_made, 1)
            pool.memset(EPS1[:, :], EPS).then_inc(consts_made, 1)
            pool.memset(EPS5[:, :], LN_EPS).then_inc(consts_made, 1)
            own.mark(pool.memset(IDENT[:, :], 0.0))
            own.mark(pool.memset(TRI[:, :], 1.0))
            own.settle()
            pool.affine_select(out=IDENT[:, :], in_=IDENT[:, :], compare_op=ALU.not_equal, fill=1.0, base=0,
                               pattern=[[-1, P]], channel_multiplier=1).then_inc(ident_made, 1)
            pool.affine_select(out=TRI[:, :], in_=TRI[:, :], compare_op=ALU.is_ge, fill=0.0, base=0,
                               pattern=[[1, S]], channel_multiplier=-1).then_inc(ident_made, 1)
            own.mark(pool.memset(MASK[:, :], 0.0))
            own.settle()
            for a in (0, 256):
                pool.affine_select(out=MASK[:, a:a + P], in_=MASK[:, a:a + P], compare_op=ALU.is_ge, fill=-3.0e38,
                                   base=0, pattern=[[-1, P]], channel_multiplier=1).then_inc(ident_made, 1)
            pool.wait_ge(x_landed[3], 16)
            pool.dma_start(VEC[:, NFIRST:NVEC], w["vec"][:, NFIRST:NVEC]).then_inc(vec_rest_landed, 16)
            pool.wait_ge(chunk_used, C_XL + RING)
            pool.dma_start(WST[:, :, :], w["gm_ws_2"]).then_inc(ws_landed, 16)
            pool.dma_start(VGB[:, :, :], w["gm_v_rows"].to_broadcast([P, 2 * 8 * P])
                           .rearrange("p (n d) -> p n d", n=2)).then_inc(vgb_landed, 16)
            pool.wait_ge(sq_added, 16)
            pool.dma_start(BSR[:, :], w["gm_bs_2"]).then_inc(bs_landed, 16)
            pool.wait_ge(ws_landed, 16)
            pool.affine_select(out=WST[:, :, :], in_=WST[:, :, :], compare_op=ALU.is_ge, fill=0.0, base=0,
                               pattern=[[0, 8], [1, P]], channel_multiplier=-1).then_inc(ws_masked, 1)
            pool.sem_inc(lru_acc, 2)
            with pool.Fori(0, 4) as i:
                for n in range(2):
                    pool.wait_ge(lru_acc, i * 2 + (n + 1))
                    pool.dma_start(WAX[:, n, 0, :], w["lru_wa_2"][:, bass.ds(i * 2 + n, 1), :]
                                   ).then_inc(wax_landed, 16)
                    pool.dma_start(WAX[:, n, 1, :], w["lru_wx_2"][:, bass.ds(i * 2 + n, 1), :]
                                   ).then_inc(wax_landed, 16)
                    pool.wait_ge(wax_landed, i * 64 + 32 * (n + 1))
            for k in range(0, 8, 4):
                pool.wait_ge(lru_q, k + 4)
                pool.tensor_scalar(QQ[:, k:k + 4, :], QQ[:, k:k + 4, :], 0.0, None, ALU.min).then_inc(lru_clamped, 1)

        @block.tensor
        def _(pe):
            def group(c, j, g, buf, moving, kts=(4, 4, 4, 4), strong=False, ready=None, hooks=None):
                pe.wait_ge(acc_evacuated, g + (2 if strong else 1))
                k, total = 0, sum(kts)
                for n, kt in enumerate(kts):
                    if ready is not None:
                        ready(n, k + kt)
                    pe.wait_ge(lo_ready, c + (j + n + 1 + RING))
                    slot = (j + n) % RING
                    for t in range(kt):
                        for m in range(2):
                            cols = slice(m * P, m * P + P)
                            nc.tensor.matmul(PS[:, 2 * buf + m, :], HI[:, slot, t, cols], moving[:, k, :],
                                             start=(k == 0), stop=False)
                            mm = nc.tensor.matmul(PS[:, 2 * buf + m, 0:S], LO[:, slot, t, cols],
                                                  moving[:, k, 0:S], start=False, stop=(k == total - 1))
                        k += 1
                    mm.then_inc(chunk_used, 1)
                    for hook in (hooks or {}).get(n, ()):
                        hook()

            def partition_sums(out, parts, signal):
                for n, part in enumerate(parts):
                    mm = nc.tensor.matmul(out, ONES[:, :], part, start=(n == 0), stop=(n == len(parts) - 1))
                mm.then_inc(signal, 1)

            def norm_sums(n):
                pe.wait_ge(sq_added, 8 * n)
                partition_sums(PS[:, 7, 0:S], [SQSUM[:, m, :] for m in range(2)], norm_acc)

            def normed(n):
                return lambda _, k: pe.wait_ge(nlo_ready, KD * n + k)

            pe.sem_inc(chunk_used, RING)

            def first_norm_sums():
                pe.wait_ge(consts_made, 3)
                for q in range(4):
                    pe.wait_ge(sq_summed, q + 1)
                    mm = nc.tensor.matmul(PS[:, 7, 0:S], ONES[:, :], SQQ[:, q, :], start=(q == 0), stop=(q == 3))
                mm.then_inc(norm_acc, 1)

            def gate_products():
                pe.wait_ge(wg_lo, 1)
                for k in range(KD):
                    nc.tensor.matmul(PS[0:16, 4, :], WGH[:, k, :], YHL[:, k, :], start=(k == 0), stop=False)
                    mm = nc.tensor.matmul(PS[0:16, 4, 0:S], WGL[:, k, :], YHL[:, k, 0:S], start=False,
                                          stop=(k == KD - 1))
                mm.then_inc(gates_acc, 1)

            def turn_gates():
                pe.wait_ge(gates_ready, 1)
                pe.wait_ge(ident_made, 1)
                for tb in range(2):
                    mm = nc.tensor.transpose(PS[:, 5, 16 * tb:16 * tb + 16], GZR[:, tb * P:tb * P + P],
                                             IDENT[0:16, 0:16])
                mm.then_inc(gates_turned, 1)

            def cumulate():
                pe.wait_ge(logf_ready, 3)
                pe.wait_ge(ident_made, 2)
                nc.tensor.matmul(PS[:, 6, 0:NG], TRI[:, 0:P], LF[:, 0, :], start=True, stop=True)
                nc.tensor.matmul(PS[:, 6, 16:16 + NG], TRI[:, P:S], LF[:, 0, :], start=True, stop=False)
                nc.tensor.matmul(PS[:, 6, 16:16 + NG], TRI[:, 0:P], LF[:, 1, :], start=False, stop=True)
                nc.tensor.matmul(PS[0:NG, 7, 0:S], NLF[:, 0, :], TRI[:, :], start=True, stop=False)
                nc.tensor.matmul(PS[0:NG, 7, P:S], NLF[:, 1, :], TRI[:, 0:P], start=False, stop=False)
                nc.tensor.matmul(PS[0:NG, 7, 0:P], GI[:, 0, :], IDENT[:, :], start=False, stop=False)
                nc.tensor.matmul(PS[0:NG, 7, P:S], GI[:, 1, :], IDENT[:, :], start=False, stop=True
                                 ).then_inc(cum_acc, 1)

            def add_logits(m, bank, signal):
                for out, qs, ks in ((PS[:, bank, 0:P], slice(0, P), slice(0, P)),
                                    (PS[:, bank, P:384], slice(P, S), slice(0, S))):
                    nc.tensor.matmul(out, QT[:, m, qs], KTT[:, m, ks], start=True, stop=False)
                    mm = nc.tensor.matmul(out, ONES[0:NG, :], RSEL[:, m, ks], start=False, stop=True)
                mm.then_inc(signal, 1)

            def transpose_v(m, bank, signal):
                for tb in range(2):
                    for t in range(2):
                        mm = nc.tensor.transpose(PS[:, bank, tb * 256 + t * P:tb * 256 + t * P + P],
                                                 VT[:, m, t, tb * P:tb * P + P], IDENT[:, :])
                mm.then_inc(signal, 1)

            def transpose_p(m, bank, signal):
                for b in range(3):
                    mm = nc.tensor.transpose(PS[:, bank, b * P:b * P + P], LG[:, m, b * P:b * P + P], IDENT[:, :])
                mm.then_inc(signal, 1)

            def weigh_v(out0, vm, cols, pm):
                nc.tensor.matmul(out0, VTOK[:, vm, 0, cols], PTS[:, pm, 0:S], start=True, stop=False)
                return nc.tensor.matmul(out0[:, P:S], VTOK[:, vm, 1, cols], PTS[:, pm, S:384], start=False, stop=True)

            def fox_sums(i, first):
                def hook():
                    if not first:
                        pe.wait_ge(vtok_ready, i)
                    else:
                        pe.wait_ge(cum_ready, 2)
                    for n in range(2):
                        pe.wait_ge(sq_ready, i * 2 + (n + 1))
                        for m in range(2):
                            for tb in range(2):
                                j = 4 * n + 2 * m + tb
                                mm = nc.tensor.matmul(PS[:, 6, j:j + 1], SQ[:, n, m, tb * P:tb * P + P],
                                                      ONES[:, 0:1], start=True, stop=True)
                    mm.then_inc(col_sums, 1)
                return hook

            def fox_spread(i, first):
                def hook():
                    pe.wait_ge(dg_ready, i + 1)
                    if not first:
                        pe.wait_ge(alo_ready, i)
                    for n in range(2):
                        mm = nc.tensor.matmul(PS[:, 6 + n, :], ONES[:, :], DG[:, 2 * n:2 * n + 2, :, :],
                                              start=True, stop=True)
                    mm.then_inc(sums_ready, 1)
                return hook

            def fox_logits(i, first):
                def hook():
                    pe.wait_ge(qk_normed, i + 1)
                    if not first:
                        pe.wait_ge(pts_ready, i * 2)
                    for m in range(2):
                        add_logits(m, 4 + m, logits_ready)
                return hook

            def fox_transposes(i):
                def hook():
                    pe.wait_ge(scaled, i * 3 + (Z_FOX + 3))
                    transpose_v(0, 6, vtr_ready)
                    for m in range(2):
                        pe.wait_ge(prob_ready, i * 2 + (m + 1))
                        transpose_p(m, 4 + m, ptr_ready)
                return hook

            def fox_weigh(i):
                def hook():
                    pe.wait_ge(vtok_ready, i + 1)
                    pe.wait_ge(pts_ready, i * 2 + 2)
                    for m in range(2):
                        mm = weigh_v(PS[:, 7, m * S:m * S + S], 0, slice(m * P, m * P + P), m)
                    mm.then_inc(pv_ready, 1)
                return hook

            def fox(i, first):
                c, g = C_FOX + i * 12, G_FOX + i * 3
                if first:
                    group(c, 0, g, 0, YHL, ready=normed(0), hooks={3: [gate_products, first_norm_sums]})
                    group(c, 4, g + 1, 1, YHL, hooks={1: [turn_gates], 3: [cumulate]})
                else:
                    group(c, 0, g, 0, YHL, strong=True, hooks={3: [fox_transposes(i - 1)]})
                    group(c, 4, g + 1, 1, YHL, hooks={1: [fox_weigh(i - 1)]})
                group(c, 8, g + 2, 0, YHL, hooks={0: [fox_sums(i, first)], 2: [fox_spread(i, first)],
                                                  3: [fox_logits(i, first)]})

            fox(0, True)
            with pe.Fori(0, 3) as i:
                fox(i + 1, False)

            def ml_scores(i):
                def hook():
                    pe.wait_ge(scaled, Z_ML + 6 * i + 2)
                    if i == 0:
                        pe.wait_ge(alo_ready, 4)
                    else:
                        pe.wait_ge(m_rt, 2 * i)
                        pe.wait_ge(m_hm, 2 * i)
                    pe.wait_ge(rsel_ready, 2 * (4 + i) + 2)
                    for m in range(2):
                        for out, ks in ((PS[:, 4 + m, 0:P], slice(0, P)), (PS[:, 4 + m, P:384], slice(0, S))):
                            mm = nc.tensor.matmul(out, ONES[0:NG, :], RSEL[:, m, ks], start=True, stop=True)
                        mm.then_inc(m_rows, 1)
                        for out, qs, ks in ((PS[:, 6 + m, 0:P], slice(0, P), slice(0, P)),
                                            (PS[:, 6 + m, P:384], slice(P, S), slice(0, S))):
                            mm = nc.tensor.matmul(out, QT[:, m, qs], KTT[:, m, ks], start=True, stop=True)
                        mm.then_inc(m_qk, 1)
                return hook

            def ml_transposes(i, m):
                def hook():
                    pe.wait_ge(scaled, Z_ML + 6 * i + 3 + m)
                    pe.wait_ge(m_prob, 2 * i + m + 1)
                    transpose_v(m, 4 + m, m_vtr)
                    transpose_p(m, 6 + m, m_ptr)
                return hook

            def ml_weigh(i, m):
                def hook():
                    pe.wait_ge(m_vtok, 2 * i + m + 1)
                    pe.wait_ge(m_pts, 2 * i + m + 1)
                    for t in range(2):
                        mm = weigh_v(PS[:, 4 + m, t * S:t * S + S], m, slice(t * P, t * P + P), m)
                    mm.then_inc(m_pv, 1)
                return hook

            def ml_sums(i):
                def hook():
                    for m in range(2):
                        pe.wait_ge(m_sq, 2 * i + m + 1)
                        partition_sums(PS[:, 6 + m, 0:S], [SQ[:, m, t, :] for t in range(2)], m_sums)
                return hook

            for i in range(2):
                c, g = C_ML + 24 * i, G_ML + 6 * i
                group(c, 0, g, 1, YHL, hooks={3: [fox_transposes(3)]} if i == 0 else {2: [ml_sums(0)]})
                group(c, 4, g + 1, 0, YHL, hooks={1: [fox_weigh(3)]} if i == 0 else None)
                group(c, 8, g + 2, 1, YHL, hooks={1: [ml_scores(i)]})
                group(c, 12, g + 3, 0, YHL, hooks={2: [ml_transposes(i, 0)]})
                group(c, 16, g + 4, 1, YHL, hooks={1: [ml_weigh(i, 0)], 2: [ml_transposes(i, 1)]})
                group(c, 20, g + 5, 0, YHL, hooks={1: [ml_weigh(i, 1)]})

            def merge(i, first):
                c, g = C_MG + i * 12, G_MG + i * 4
                group(c, 0, g, 1, YHL, hooks={2: [ml_sums(1)]} if first else None)
                group(c, 4, g + 1, 0, YHL)
                if first:
                    pe.wait_ge(alo_ready, 4)
                group(c, 8, g + 2, 1, AHL[:, 0:8], (4, 4))
                if first:
                    pe.wait_ge(m_alo, 4)
                group(c, 10, g + 3, 0, AHL[:, 8:16], (4, 4))

            merge(0, True)
            with pe.Fori(0, 7) as i:
                merge(i + 1, False)

            def square(c0, g0, moving, kts, ready, hooks=None):
                per = len(kts)
                group(c0, 0, g0, 1, moving, kts, ready=ready, hooks=hooks)
                group(c0, per, g0 + 1, 0, moving, kts)
                with pe.Fori(1, 4) as i:
                    for n in range(2):
                        group(c0 + i * (2 * per), n * per, g0 + i * 2 + n, 1 - n, moving, kts)

            def up(c0, g0, ff, n):
                group(c0, 0, g0, 1, YHL, ready=normed(n), hooks={1: [lambda: norm_sums(n)]})
                group(c0, 4, g0 + 1, 0, YHL)
                with pe.Fori(1, ff // GROUP) as i:
                    group(c0 + i * 8, 0, g0 + i * 2, 1, YHL)
                    group(c0 + i * 8, 4, g0 + i * 2 + 1, 0, YHL)

            K4 = (4, 4, 4, 4)
            square(C_OUT, G_OUT, MHL, K4, lambda _, k: pe.wait_ge(mlo_ready, k // 2))
            up(C_UP, G_UP, FF1, 1)
            square(C_DN, G_DN, H, KT1, lambda _, k: pe.wait_ge(hlo_ready, (k + 1) // 2))

            group(C_XL, 0, G_XL, 1, YHL, ready=normed(2), hooks={1: [lambda: norm_sums(2)]})
            group(C_XL, 4, G_XL + 1, 0, YHL)
            group(C_XL, 8, G_XL + 2, 1, YHL)
            group(C_XL, 12, G_XL + 3, 0, YHL)

            def lru_gate_products(s):
                def hook():
                    for m in range(2):
                        k = 2 * s + m
                        pe.wait_ge(wax_landed, k * 32 + 32)
                        pe.wait_ge(xr_ready, 6 * (s + 1))
                        if s > 0:
                            pe.wait_ge(lru_gates, 2 * (k - 1))
                        for a in range(2):
                            mm = nc.tensor.matmul(PS[:, 4 + m, a * S:a * S + S], WAX[:, m, a, :], HL[:, k, :],
                                                  start=True, stop=True)
                        mm.then_inc(lru_acc, 1)
                return hook

            def turn_v(s):
                def hook():
                    pe.wait_ge(v_gelu, s + 1)
                    if s > 0:
                        pe.wait_ge(v_tokens, 2 * s)
                    for b in range(2):
                        for m in range(2):
                            mm = nc.tensor.transpose(PS[:, 6, (2 * b + m) * P:(2 * b + m) * P + P],
                                                     ST[:, m, b * P:b * P + P], IDENT[:, :])
                    mm.then_inc(v_turned, 1)
                return hook

            def mix(q):
                def hook():
                    if q == 0:
                        pe.wait_ge(ws_masked, 1)
                        pe.wait_ge(bs_landed, 16)
                    pe.wait_ge(vn_ready, 2 * (q + 1))
                    if q >= 2:
                        pe.wait_ge(mixed_ready, q - 1)
                    for m in range(2):
                        h = 2 * q + m
                        for b in range(2):
                            out = PS[:, 7 - q % 2, m * S + b * P:m * S + b * P + P]
                            nc.tensor.matmul(out, VTB[:, b, h, :], WST[:, h, :], start=True, stop=False)
                            mm = nc.tensor.matmul(out, ONES[0:1, :], BSR[0:1, h * P:h * P + P],
                                                  start=False, stop=True)
                    mm.then_inc(mix_acc, 1)
                return hook

            def gm_sums():
                pe.wait_ge(gm_sq, 1)
                partition_sums(PS[:, 4, 0:S], [SQG[:, k, :] for k in range(8)], gm_acc)

            def lru_sums():
                for k in range(8):
                    if k % 2 == 0:
                        pe.wait_ge(lru_sq, k // 2 + 1)
                    mm = nc.tensor.matmul(PS[:, 5, 0:S], ONES[:, :], SQL[:, k, :], start=(k == 0), stop=(k == 7))
                mm.then_inc(lru_sums_acc, 1)

            for s in range(4):
                group(C_V, 4 * s, G_V + s, 1 - s % 2, YHL, hooks={3: [turn_v(s - 1)]} if s > 0 else None)
            for s in range(4):
                group(C_U, 4 * s, G_U + s, 1 - s % 2, YHL,
                      hooks={1: [lru_gate_products(s)], 3: [turn_v(3)] if s == 0 else []})
            for s, hooks in enumerate(({3: [mix(0), mix(1)]}, {2: [mix(2), mix(3)]}, {1: [gm_sums]}, None)):
                group(C_GL, 4 * s, G_GL + s, 1 - s % 2, YHL, hooks=hooks)

            square(C_O2, G_O2, AHL, K4, lambda _, k: pe.wait_ge(out_lo_ready, k // 2), {0: [lru_sums]})
            up(C_U2, G_U2, FF2, 3)
            square(C_D2, G_D2, H, KT2, lambda _, k: pe.wait_ge(hlo_ready, 22 + (k + 1) // 2))
            norm_sums(4)

        @block.scalar
        def _(act):
            def hi(c, j, kt=4):
                s = j % RING
                act.wait_ge(raw_landed[s], c * 4 + 16 * (j // RING + 1))
                act.wait_ge(chunk_used, c + (j + 1))
                nc.scalar.activation(HI[:, s, 0:kt, :], RAW[:, s, 0:kt, :], ACT.Copy).then_inc(hi_ready, 1)

            def splits(c, a, b, kts=()):
                for j in range(a, b):
                    hi(c, j, kts[j] if j < len(kts) else 4)

            def norm_root_of(n):
                act.wait_ge(norm_acc, n + 1)
                nc.scalar.activation(RSTD[:, :], PS[:, 7, 0:S], ACT.Sqrt, bias=EPS1[:, :], scale=1.0 / D
                                     ).then_inc(norm_root, 1)

            def gain_hi(name, k, vk):
                nc.scalar.activation(YHL[:, at_tile(k), 0:S], X[:, at_tile(k), :], ACT.Copy,
                                     scale=VEC[:, at_tile(vk, COL[name])]).then_inc(nhi_ready, 1)

            for q in (0, 1):
                nc.scalar.dma_start(X[:, 4 * q:4 * q + 4, :], w["x"][:, 4 * q:4 * q + 4, :]).then_inc(x_landed[q], 16)
            act.wait_ge(vec_landed, 16)
            for q in range(4):
                act.wait_ge(x_landed[q], 16)
                for k in range(4 * q, 4 * q + 4):
                    gain_hi("norm1_g", k, k)
                splits(C_FOX, q, q + 1)
            act.wait_ge(gate_w_landed, 16)
            nc.scalar.activation(WGH[:, :, :], WG[:, :, :], ACT.Copy).then_inc(wg_hi, 1)
            for q in range(4):
                nc.scalar.activation(XSQ[:, 4 * q:4 * q + 4, :], X[:, 4 * q:4 * q + 4, :], ACT.Square
                                     ).then_inc(x_squared, 1)
            splits(C_FOX, 4, 8)
            act.wait_ge(consts_made, 3)
            norm_root_of(0)

            def gate_logs():
                act.wait_ge(gate_abs, 1)
                nc.scalar.activation(GE[:, :, :], GA_[:, :, :], ACT.Exp, scale=-1.0).then_inc(gate_exp, 1)
                act.wait_ge(gate_exp, 1)
                nc.scalar.activation(GE[:, :, :], GE[:, :, :], ACT.Ln, bias=ONES[:, 0:1]).then_inc(gate_ln, 1)

            def exps(m, signal, sums):
                for b, cols in enumerate((slice(0, P), slice(P, 384))):
                    ins = nc.scalar.activation(LG[:, m, cols], LG[:, m, cols], ACT.Exp, bias=NM[:, m, b:b + 1],
                                               **({"accum_out": RS[:, m, b:b + 1]} if sums else {}))
                    ins.then_inc(signal, 1)

            def fox_copies(i):
                act.wait_ge(vtr_ready, i + 1)
                nc.scalar.activation(VTOK[:, 0, :, :], PS[:, 6, :].rearrange("p (b n) -> p b n", b=2), ACT.Copy
                                     ).then_inc(vtok_ready, 1)
                for m in range(2):
                    act.wait_ge(ptr_ready, i * 2 + (m + 1))
                    nc.scalar.activation(PTS[:, m, :], PS[:, 4 + m, 0:384], ACT.Copy).then_inc(pts_ready, 1)

            def fox_out_hi(i):
                act.wait_ge(pv_ready, i + 1)
                nc.scalar.activation(AHL[:, bass.ds(i * 2, 2), 0:S], PS[:, 7, :].rearrange("p (m n) -> p m n", m=2),
                                     ACT.Copy).then_inc(ahi_ready, 1)

            def fox(i, first):
                c = C_FOX + i * 12
                if not first:
                    splits(c, 5, 7)
                if first:
                    gate_logs()
                act.wait_ge(scaled, i * 3 + (Z_FOX + 1))
                nc.scalar.activation(SQ[:, 0, :, :], QT[:, :, :], ACT.Square).then_inc(sq_ready, 1)
                if first:
                    splits(c, 8, 11)
                else:
                    fox_copies(i - 1)
                    splits(c, 7, 11)
                if not first:
                    fox_out_hi(i - 1)
                act.wait_ge(scaled, i * 3 + (Z_FOX + 2))
                nc.scalar.activation(SQ[:, 1, :, :], KTT[:, :, :], ACT.Square).then_inc(sq_ready, 1)
                splits(c, 11, 12)
                act.wait_ge(col_sums, i + 1)
                nc.scalar.activation(RCOL[:, :], PS[:, 6, 0:8], ACT.Sqrt, bias=EPS1[:, :], scale=1.0 / FOX_HD
                                     ).then_inc(col_roots, 1)
                splits(c, 12, 15)
                for m in range(2):
                    act.wait_ge(negmax_ready, i * 2 + (m + 1))
                    exps(m, exp_ready, True)
                splits(c, 15, 17)

            fox(0, True)
            with act.Fori(0, 3) as i:
                fox(i + 1, False)

            def ml_exps(i, m):
                act.wait_ge(m_negmax, 2 * i + m + 1)
                exps(m, m_exp, False)
                nc.scalar.activation(EM[:, m, :], NM[:, m, :], ACT.Exp).then_inc(m_exp, 1)

            def ml_copies(i, m):
                act.wait_ge(m_vtr, 2 * i + m + 1)
                nc.scalar.activation(VTOK[:, m, :, :], PS[:, 4 + m, :].rearrange("p (b n) -> p b n", b=2), ACT.Copy
                                     ).then_inc(m_vtok, 1)
                act.wait_ge(m_ptr, 2 * i + m + 1)
                nc.scalar.activation(PTS[:, m, :], PS[:, 6 + m, 0:384], ACT.Copy).then_inc(m_pts, 1)

            def ml_roots(i):
                for m in range(2):
                    act.wait_ge(m_sums, 2 * i + m + 1)
                    nc.scalar.activation(RT[:, m, 0, :], PS[:, 6 + m, 0:S], ACT.Sqrt, bias=EPS1[:, :],
                                         scale=1.0 / ML_DV).then_inc(m_rt, 1)

            def ml_out_hi(i, m):
                act.wait_ge(m_out, 2 * i + m + 1)
                nc.scalar.activation(AHL[:, 8 + 4 * i + 2 * m:10 + 4 * i + 2 * m, 0:S], HM[:, m, :, :],
                                     ACT.Copy).then_inc(m_ahi, 1)

            for i in range(2):
                c = C_ML + 24 * i
                if i == 1:
                    ml_roots(0)
                splits(c, 5, 7)
                if i == 0:
                    fox_copies(3)
                splits(c, 7, 9)
                if i == 1:
                    ml_out_hi(0, 0)
                splits(c, 9, 11)
                if i == 1:
                    ml_out_hi(0, 1)
                if i == 0:
                    fox_out_hi(3)
                splits(c, 11, 12)
                ml_exps(i, 0)
                splits(c, 12, 16)
                ml_exps(i, 1)
                splits(c, 16, 18)
                ml_copies(i, 0)
                splits(c, 18, 22)
                ml_copies(i, 1)
                splits(c, 22, 23)
                for m in range(2):
                    if m == 1:
                        splits(c, 23, 27)
                    act.wait_ge(scaled, Z_ML + 6 * i + 5 + m)
                    nc.scalar.activation(MO[:, m, :, :], MO[:, m, :, :], ACT.Sigmoid).then_inc(m_gate, 1)
                    act.wait_ge(m_hm, 2 * i + m + 1)
                    nc.scalar.activation(SQ[:, m, :, :], HM[:, m, :, :], ACT.Square).then_inc(m_sq, 1)
                splits(c, 27, 29)

            def merge(i, first):
                c = C_MG + i * 12
                if first:
                    ml_roots(1)
                splits(c, 5, 7)
                for n in range(2):
                    act.wait_ge(scaled, i * 2 + (Z_MG + n + 1))
                    nc.scalar.activation(SG[:, n, :, :], SG[:, n, :, :], ACT.Sigmoid).then_inc(sg_ready, 1)
                    if n == 0:
                        splits(c, 7, 9)
                        if first:
                            ml_out_hi(1, 0)
                        splits(c, 9, 11)
                        if first:
                            ml_out_hi(1, 1)
                splits(c, 11, 15)
                splits(c, 15, 16)
                act.wait_ge(merged_ready, i + 1)
                nc.scalar.activation(MHL[:, bass.ds(i * 2, 2), 0:S], T1[:, :, :], ACT.Copy).then_inc(mhi_ready, 1)
                splits(c, 16, 17)

            merge(0, True)
            with act.Fori(0, 7) as i:
                merge(i + 1, False)

            def square(c0, kts, n, name):
                per = len(kts)

                def body(i, final=False):
                    c = c0 + i * (2 * per)
                    for h in range(2):
                        end = (h + 1) * per
                        stop = end + (0 if final and h else 5)
                        splits(c, 5 + h * per, min(end + 4, stop), kts + kts)
                        act.wait_ge(x_added, i * 2 + (8 * (n - 1) + h + 1))
                        nc.scalar.activation(YC[:, 2:4, :], X[:, bass.ds(i * 4 + 2 * h, 2), :], ACT.Square
                                             ).then_inc(x_squared, 1)
                        for k in range(2):
                            if name is not None:
                                gain_hi(name, i * 4 + (2 * h + k), i * 4 + (2 * h + k))
                            elif not (final and h):
                                act.wait_ge(x_squared, i * 2 + (4 + 8 * (n - 1) + h + 1))
                                x = X[:, bass.ds(i * 4 + (2 * h + k), 1), :]
                                nc.scalar.activation(x, x, ACT.Copy, scale=VEC[:, at_tile(
                                    i * 4 + (2 * h + k), COL["final_g_2"])]).then_inc(xg_ready, 1)
                        splits(c, min(end + 4, stop), stop, kts + kts)

                last = name is None
                with act.Fori(0, 3 if last else 4) as i:
                    body(i)
                if last:
                    body(3, True)

            def up(c0, z0, ff, it0, n, cw, cb, func):
                tiles = ff // P

                def tap(z, side, col):
                    act.wait_ge(scaled, z)
                    for m in range(2):
                        nc.scalar.activation(YC[:, 2 * side + m, :], UP[:, side, m, 2:S + 2], ACT.Identity,
                                             scale=VEC[:, bass.ds(col + (COL[cw] + 2 * 2 * tiles + m), 1)],
                                             bias=VEC[:, bass.ds(col + (COL[cb] + m), 1)]).then_inc(tap_ready, 1)

                def body(i, first):
                    c, z = c0 + i * 8, z0 + i * 2
                    if first:
                        norm_root_of(n)
                    splits(c, 5, 8)
                    tap(z + 1, 0, i * 2)
                    splits(c, 8, 11)
                    act.wait_ge(conv_ready, i * 8 + (8 * it0 + 4))
                    nc.scalar.activation(YC[:, 0:2, :], YC[:, 0:2, :], func).then_inc(gate_act, 1)
                    splits(c, 11, 12)
                    tap(z + 2, 1, i * 2 + tiles)
                    splits(c, 12, 13)
                    act.wait_ge(hid_ready, i + (it0 + 1))
                    nc.scalar.activation(H[:, bass.ds(i * 2, 2), 0:S], YC[:, 0:2, :], ACT.Copy).then_inc(hhi_ready, 1)

                body(0, True)
                with act.Fori(1, ff // GROUP) as i:
                    body(i, False)

            act.wait_ge(vec_rest_landed, 16)
            square(C_OUT, [4] * 4, 1, "norm2_g")
            up(C_UP, Z_UP, FF1, 0, 1, "conv_w", "conv_b", ACT.Silu)
            square(C_DN, KT1, 2, "norm1_g_2")

            act.wait_ge(c8_abs, 1)
            nc.scalar.activation(C8W[:, 0, :], C8W[:, 1, :], ACT.Exp, scale=-1.0).then_inc(c8_exp, 1)
            act.wait_ge(c8_exp, 1)
            nc.scalar.activation(C8W[:, 0, :], C8W[:, 0, :], ACT.Ln, bias=ONES[:, 0:1]).then_inc(c8_ln, 1)
            norm_root_of(2)
            splits(C_XL, 5, 21)

            def lru_tap(k):
                nc.scalar.activation(HL[:, k, :], XL[:, k, 3:S + 3], ACT.Identity,
                                     scale=VEC[:, COL["lru_conv_w_2"] + 24 + k:COL["lru_conv_w_2"] + 25 + k],
                                     bias=VEC[:, COL["lru_conv_b_2"] + k:COL["lru_conv_b_2"] + k + 1]
                                     ).then_inc(xr_tap, 1)

            def v_to_tokens(s):
                act.wait_ge(v_turned, s + 1)
                for b in range(2):
                    nc.scalar.activation(VTB[:, b, 2 * s:2 * s + 2, :].rearrange("p h d -> p (h d)"),
                                         PS[:, 6, b * 256:b * 256 + 256], ACT.Copy,
                                         accum_out=VSUM[:, b, s:s + 1]).then_inc(v_tokens, 1)

            for s in range(4):
                c = C_V + 4 * s
                splits(c, 5, 6)
                act.wait_ge(scaled, Z_XL + s + 1)
                for m in range(2):
                    lru_tap(2 * s + m)
                splits(c, 6, 8)
                if s > 0:
                    v_to_tokens(s - 1)
                act.wait_ge(scaled, Z_V + s + 1)
                nc.scalar.activation(ST[:, :, :], ZT[:, :, :], ACT.Gelu_apprx_tanh).then_inc(v_gelu, 1)
                splits(c, 8, 9)

            def lru_gates_of(k):
                m = k % 2
                act.wait_ge(lru_acc, k + (1 + 2))
                act.wait_ge(c8_ready, 3)
                if k >= 2:
                    act.wait_ge(lru_q, k - 1)
                for a in range(2):
                    nc.scalar.activation(RI[:, m, a, :], PS[:, 4 + m, a * S:a * S + S], ACT.Tanh, scale=0.5,
                                         bias=HB[:, 8 * a + k:8 * a + k + 1]).then_inc(lru_gates, 1)
                act.wait_ge(lru_gates, 2 * k + 1)
                half, full = C8H[:, k:k + 1], C8[:, k:k + 1]
                nc.scalar.activation(AA[:, k, :], RI[:, m, 0, :], ACT.Exp, scale=half, bias=half).then_inc(lru_th, 1)
                nc.scalar.activation(LA2[:, m, :], RI[:, m, 0, :], ACT.Exp, scale=full, bias=full).then_inc(lru_th, 1)
                nc.scalar.activation(LT[:, m, :], RI[:, m, 0, :], ACT.Tanh, scale=half, bias=half).then_inc(lru_th, 1)

            for s in range(4):
                c = C_U + 4 * s
                splits(c, 5, 6)
                lru_gates_of(2 * s)
                splits(c, 6, 7)
                lru_gates_of(2 * s + 1)
                splits(c, 7, 8)
                if s == 0:
                    v_to_tokens(3)
                splits(c, 8, 9)
                if s == 0:
                    act.wait_ge(ln_mean, 1)
                    for b in range(2):
                        if b == 1:
                            act.wait_ge(ln_sq, 1)
                        nc.scalar.activation(GZ[:, 4:8, :].rearrange("p k n -> p (k n)"),
                                             VTB[:, b, :, :].rearrange("p h d -> p (h d)"), ACT.Square,
                                             bias=NMEAN[:, b:b + 1], accum_out=VSQ[:, b:b + 1]).then_inc(ln_sq, 1)
                    act.wait_ge(ln_sq, 2)
                    nc.scalar.activation(VSQ[:, :], VSQ[:, :], ACT.Sqrt, bias=EPS5[:, :], scale=1.0 / 1024
                                         ).then_inc(ln_root, 1)

            def square_pair(q):
                act.wait_ge(lru_gated, q + 1)
                nc.scalar.activation(SQL[:, 2 * q:2 * q + 2, :], HL[:, 2 * q:2 * q + 2, :], ACT.Square
                                     ).then_inc(lru_sq, 1)

            def out_hi(q):
                act.wait_ge(out_gained, 2 * q + 2)
                src = GZ if q < 4 else HL
                nc.scalar.activation(AHL[:, 2 * q:2 * q + 2, 0:S], src[:, 2 * (q % 4):2 * (q % 4) + 2, :], ACT.Copy
                                     ).then_inc(out_hi_ready, 1)

            for s in range(4):
                c = C_GL + 4 * s
                splits(c, 5, 6)
                if s == 0:
                    for k in (0, 4):
                        act.wait_ge(lru_clamped, k // 4 + 1)
                        nc.scalar.activation(QQ[:, k:k + 4, :], QQ[:, k:k + 4, :], ACT.Sqrt, scale=-0.25
                                             ).then_inc(lru_mult, 1)
                if s == 2:
                    act.wait_ge(gm_acc, 1)
                    nc.scalar.activation(MU[:, :], PS[:, 4, 0:S], ACT.Sqrt, bias=EPS1[:, :], scale=1.0 / 1024
                                         ).then_inc(gm_root, 1)
                if s == 3:
                    out_hi(1)
                    out_hi(2)
                splits(c, 6, 8)
                if s == 0:
                    act.wait_ge(scaled, Z_U + 4)
                    nc.scalar.activation(GZ[:, :, :], GZ[:, :, :], ACT.Gelu_apprx_tanh).then_inc(u_gelu, 1)
                act.wait_ge(scaled, Z_GL + s + 1)
                nc.scalar.activation(GL[:, 2 * s:2 * s + 2, :], GL[:, 2 * s:2 * s + 2, :], ACT.Gelu_apprx_tanh
                                     ).then_inc(g_gelu, 1)
                if s == 1:
                    act.wait_ge(mixed_ready, 4)
                    nc.scalar.activation(SQG[:, :, :], GZ[:, :, :], ACT.Square).then_inc(gm_sq, 1)
                if s == 2:
                    for q in range(3):
                        square_pair(q)
                    out_hi(0)
                if s == 3:
                    square_pair(3)
                    out_hi(3)
                else:
                    splits(c, 8, 9)
            act.wait_ge(lru_sums_acc, 1)
            nc.scalar.activation(RSTD[:, :], PS[:, 5, 0:S], ACT.Sqrt, bias=EPS1[:, :], scale=1.0 / 1024
                                 ).then_inc(lru_root, 1)
            for q in range(4, 8):
                out_hi(q)
            splits(C_O2, 4, 5)

            square(C_O2, [4] * 4, 3, "norm2_g_2")
            up(C_U2, Z_U2, FF2, 22, 3, "ffn_conv_w_2", "ffn_conv_b_2", ACT.Gelu_apprx_tanh)
            square(C_D2, KT2, 4, None)
            norm_root_of(4)

        @block.vector
        def _(dve):
            own = Chain(dve, dve_own)

            def lo(c, j, kt=4):
                s = j % RING
                dve.wait_ge(hi_ready, c + (j + 1))
                nc.vector.tensor_tensor(LO[:, s, 0:kt, :], RAW[:, s, 0:kt, :], HI[:, s, 0:kt, :].bitcast(F32),
                                        ALU.subtract).then_inc(lo_ready, 1)

            def splits(c, a, b, kts=()):
                for j in range(a, b):
                    lo(c, j, kts[j] if j < len(kts) else 4)

            def evacuate(c, end, buf, out):
                dve.wait_ge(chunk_used, c + (end + RING))
                nc.vector.tensor_reduce(out, acc(buf), AX.X, ALU.add).then_inc(acc_evacuated, 1)

            def evacuated(g):
                dve.wait_ge(acc_evacuated, g + 2)

            def tt(out, a, b, op):
                return nc.vector.tensor_tensor(out, a, b, op)

            def stt(out, a, s, b, op0, op1, **kw):
                return nc.vector.scalar_tensor_tensor(out=out, in0=a, scalar=s, in1=b, op0=op0, op1=op1, **kw)

            def vec(name, k):
                return VEC[:, COL[name] + k:COL[name] + k + 1]

            def norm_rstd(n):
                dve.wait_ge(norm_root, n + 1)
                nc.vector.reciprocal(RSTD[:, :], RSTD[:, :]).then_inc(rstd_ready, 1)
                dve.wait_ge(rstd_ready, n + 1)

            def scale(g, out):
                dve.wait_ge(acc_evacuated, g + 2)
                tt(out, out, RSTD[:, :].unsqueeze(1).to_broadcast([P, 2, S]), ALU.mult).then_inc(scaled, 1)

            def gain_lo(name, n, k):
                dve.wait_ge(nhi_ready, k + (KD * n + 1))
                stt(YHL[:, at_tile(k), S:2 * S], X[:, at_tile(k), :], VEC[:, at_tile(k, COL[name])],
                    YHL[:, at_tile(k), 0:S].bitcast(F32), ALU.mult, ALU.subtract).then_inc(nlo_ready, 1)

            dve.sem_inc(acc_evacuated, 2)

            dve.wait_ge(vec_landed, 16)
            for q in range(4):
                for k in range(4 * q, 4 * q + 4):
                    gain_lo("norm1_g", 0, k)
                splits(C_FOX, q, q + 1)
            own.mark(nc.vector.tensor_scalar(QG[:, :], vec("q_norm_g", 0), float(FOX_HD) ** -0.5, None, ALU.mult))
            dve.wait_ge(wg_hi, 1)
            tt(WGL[:, :, :], WG[:, :, :], WGH[:, :, :].bitcast(F32), ALU.subtract).then_inc(wg_lo, 1)
            for q in range(4):
                dve.wait_ge(x_squared, q + 1)
                nc.vector.tensor_reduce(SQQ[:, q, :], XSQ[:, 4 * q:4 * q + 4, :].rearrange("p k n -> p n k"),
                                        AX.X, ALU.add).then_inc(sq_summed, 1)
            splits(C_FOX, 4, 8)
            norm_rstd(0)

            def gate_rows():
                dve.wait_ge(gates_acc, 1)
                own.mark(nc.vector.tensor_reduce(GZR[:, :], PS[0:16, 4, :].rearrange("p (h n) -> p n h", h=2),
                                                 AX.X, ALU.add))
                own.settle()
                own.mark(tt(GZR[:, :], GZR[:, :], RSTD[0:16, :], ALU.mult))
                own.settle()
                dve.wait_ge(gate_b_landed, 16)
                nc.vector.tensor_scalar(GZR[:, :], GZR[:, :], GB[:, 0:1], None, ALU.add).then_inc(gates_ready, 1)

            def gates():
                dve.wait_ge(gates_turned, 1)
                own.mark(nc.vector.tensor_copy(GZT[:, :, :], PS[:, 5, 0:32].rearrange("p (b h) -> p b h", b=2)))
                own.settle()
                stt(GA_[:, :, :], GZT[:, :, :], -1.0, GZT[:, :, :], ALU.mult, ALU.max).then_inc(gate_abs, 1)
                own.mark(nc.vector.tensor_scalar(NLF[:, :, :], GZT[:, :, 0:NG], 0.0, None, ALU.min))
                own.mark(nc.vector.memset(GI[:, :, :], 0.0))
                own.settle()
                nc.vector.tensor_copy(GI[:, :, FOX_HEADS:NG], GZT[:, :, NG:16]).then_inc(logf_ready, 1)

            def log_forget():
                dve.wait_ge(logf_ready, 1)
                dve.wait_ge(gate_ln, 1)
                tt(LF[:, :, :], NLF[:, :, :], GE[:, :, 0:NG], ALU.subtract).then_inc(logf_ready, 1)
                dve.wait_ge(logf_ready, 2)
                nc.vector.tensor_scalar(NLF[:, :, :], LF[:, :, :], -1.0, None, ALU.mult).then_inc(logf_ready, 1)

            def cumulated():
                dve.wait_ge(cum_acc, 1)
                nc.vector.tensor_copy(CUM[:, :, :], PS[:, 6, 0:32].rearrange("p (b h) -> p h b", b=2)[:, 0:NG, :]
                                      ).then_inc(cum_ready, 1)
                nc.vector.tensor_copy(ROWS[:, :], PS[0:NG, 7, 0:S]).then_inc(cum_ready, 1)
                dve.wait_ge(cum_ready, 2)
                own.mark(nc.vector.tensor_scalar(NCUM[:, :, :], CUM[:, :, :], -1.0, None, ALU.mult))
                own.settle()

            def select_rows(h0):
                for m in range(2):
                    nc.vector.tensor_scalar(RSEL[:, m, :], ROWS[:, :], IDENT[0:NG, bass.ds(h0 + m, 1)], None,
                                            ALU.mult).then_inc(rsel_ready, 1)

            def fox_diagonals(i):
                dve.wait_ge(col_roots, i + 1)
                own.mark(nc.vector.reciprocal(RCOL[:, :], RCOL[:, :]))
                own.settle()
                tt(DG[:, :, :, :].rearrange("p a b d -> p (a b) d"), IDENT[:, :].unsqueeze(1).to_broadcast([P, 8, P]),
                   RCOL[:, :].unsqueeze(2).to_broadcast([P, 8, P]), ALU.mult).then_inc(dg_ready, 1)

            def fox_norm(i):
                dve.wait_ge(sums_ready, i + 1)
                dve.wait_ge(scaled, i * 3 + (Z_FOX + 2))
                dve.wait_ge(rsel_ready, i * 2 + 2)
                own.mark(stt(QT[:, :, :], QT[:, :, :], QG[:, :], PS[:, 6, :].rearrange("p (m n) -> p m n", m=2),
                             ALU.mult, ALU.mult))
                own.settle()
                stt(KTT[:, :, :], KTT[:, :, :], vec("k_norm_g", 0), PS[:, 7, :].rearrange("p (m n) -> p m n", m=2),
                    ALU.mult, ALU.mult).then_inc(qk_normed, 1)

            def masked(i, m, h, bank, cum):
                for b, cols in enumerate((slice(0, P), slice(P, 384))):
                    own.mark(stt(LG[:, m, cols], PS[:, bank, cols], cum[:, bass.ds(h, 1), b:b + 1], MASK[:, cols],
                                 ALU.add, ALU.add))
                own.settle()
                for b, cols in enumerate((slice(0, P), slice(P, 384))):
                    own.mark(nc.vector.tensor_reduce(MX[:, m, b:b + 1], LG[:, m, cols], AX.X, ALU.max))
                own.settle()

            def normalise(m, signal):
                own.mark(nc.vector.reciprocal(RS[:, m, :], RS[:, m, :]))
                own.settle()
                own.mark(nc.vector.tensor_scalar(LG[:, m, 0:P], LG[:, m, 0:P], RS[:, m, 0:1], None, ALU.mult))
                own.settle()
                nc.vector.tensor_scalar(LG[:, m, P:384], LG[:, m, P:384], RS[:, m, 1:2], None, ALU.mult
                                        ).then_inc(signal, 1)

            def fox_maxima(i):
                for m in range(2):
                    dve.wait_ge(logits_ready, i * 2 + (m + 1))
                    masked(i, m, i * 2 + m, 4 + m, CUM)
                    nc.vector.tensor_scalar(NM[:, m, :], MX[:, m, :], -1.0, None, ALU.mult).then_inc(negmax_ready, 1)

            def fox_probabilities(i):
                for m in range(2):
                    dve.wait_ge(exp_ready, i * 4 + 2 * (m + 1))
                    normalise(m, prob_ready)

            def fox_out_lo(i):
                dve.wait_ge(ahi_ready, i + 1)
                tt(AHL[:, bass.ds(i * 2, 2), S:2 * S], PS[:, 7, :].rearrange("p (m n) -> p m n", m=2),
                   AHL[:, bass.ds(i * 2, 2), 0:S].bitcast(F32), ALU.subtract).then_inc(alo_ready, 1)

            def fox(i, first):
                c, z = C_FOX + i * 12, i * 3 + G_FOX
                if first:
                    gate_rows()
                    gates()
                else:
                    splits(c, 5, 7)
                evacuate(c, 4, 0, QT[:, :, :])
                scale(z + 1, QT[:, :, :])
                if first:
                    log_forget()
                    splits(c, 8, 11)
                    dve.wait_ge(ident_made, 4)
                    cumulated()
                else:
                    splits(c, 7, 11)
                evacuate(c, 8, 1, KTT[:, :, :])
                scale(z + 2, KTT[:, :, :])
                if not first:
                    fox_out_lo(i - 1)
                splits(c, 11, 12)
                select_rows(i * 2)
                fox_diagonals(i)
                splits(c, 12, 13)
                fox_norm(i)
                splits(c, 13, 15)
                evacuate(c, 12, 0, VT[:, 0, :, :])
                scale(z + 3, VT[:, 0, :, :])
                fox_maxima(i)
                splits(c, 15, 16)
                fox_probabilities(i)
                splits(c, 16, 17)

            fox(0, True)
            with dve.Fori(0, 3) as i:
                own.enter(i, 14)
                fox(i + 1, False)
                own.leave(3)

            def ml_weights(i, m):
                h = FOX_HEADS + 2 * i + m
                dve.wait_ge(m_rows, 2 * i + m + 1)
                masked(i, m, h, 4 + m, CUM)
                stt(NM[:, m, :], MX[:, m, :], -1.0, NCUM[:, h, :], ALU.mult, ALU.min).then_inc(m_negmax, 1)
                dve.wait_ge(m_qk, 2 * i + m + 1)
                dve.wait_ge(m_exp, 3 * (2 * i + m + 1))
                for b, cols in enumerate((slice(0, P), slice(P, 384))):
                    own.mark(stt(LG[:, m, cols], PS[:, 6 + m, cols], float(ML_DQK) ** -0.5, LG[:, m, cols],
                                 ALU.mult, ALU.mult, accum_out=RS[:, m, b:b + 1]))
                own.settle()
                own.mark(tt(EM[:, m, :], RS[:, m, :], EM[:, m, :], ALU.max))
                own.settle()
                own.mark(stt(RS[:, m, :], RS[:, m, :], -1.0, EM[:, m, :], ALU.mult, ALU.max))
                own.settle()
                normalise(m, m_prob)

            def ml_out(i, m):
                dve.wait_ge(m_rt, 2 * i + m + 1)
                own.mark(nc.vector.reciprocal(RT[:, m, 0, :], RT[:, m, 0, :]))
                dve.wait_ge(m_gate, 2 * i + m + 1)
                own.settle()
                for t in range(2):
                    own.mark(stt(HM[:, m, t, :], HM[:, m, t, :], vec("m_norm_g", 4 * i + 2 * m + t),
                                 RT[:, m, 0, :], ALU.mult, ALU.mult))
                own.settle()
                tt(HM[:, m, :, :], HM[:, m, :, :], MO[:, m, :, :], ALU.mult).then_inc(m_out, 1)

            def ml_out_lo(i, m):
                dve.wait_ge(m_ahi, 2 * i + m + 1)
                ks = slice(8 + 4 * i + 2 * m, 10 + 4 * i + 2 * m)
                tt(AHL[:, ks, S:2 * S], HM[:, m, :, :], AHL[:, ks, 0:S].bitcast(F32), ALU.subtract
                   ).then_inc(m_alo, 1)

            for i in range(2):
                c, g = C_ML + 24 * i, G_ML + 6 * i
                splits(c, 5, 7)
                evacuate(c, 4, 1, QT[:, :, :])
                scale(g + 1, QT[:, :, :])
                select_rows(FOX_HEADS + 2 * i)
                if i == 1:
                    ml_out(0, 0)
                splits(c, 7, 9)
                if i == 1:
                    ml_out_lo(0, 0)
                    ml_out(0, 1)
                splits(c, 9, 11)
                if i == 1:
                    ml_out_lo(0, 1)
                if i == 0:
                    fox_out_lo(3)
                evacuate(c, 8, 0, KTT[:, :, :])
                scale(g + 2, KTT[:, :, :])
                splits(c, 11, 12)
                ml_weights(i, 0)
                splits(c, 12, 15)
                evacuate(c, 12, 1, VT[:, 0, :, :])
                scale(g + 3, VT[:, 0, :, :])
                splits(c, 15, 16)
                ml_weights(i, 1)
                splits(c, 16, 19)
                evacuate(c, 16, 0, VT[:, 1, :, :])
                scale(g + 4, VT[:, 1, :, :])
                splits(c, 19, 23)
                for m in range(2):
                    if m == 1:
                        splits(c, 23, 27)
                    evacuate(c, 20 + 4 * m, 1 - m, MO[:, m, :, :])
                    scale(g + 5 + m, MO[:, m, :, :])
                    dve.wait_ge(m_pv, 2 * i + m + 1)
                    nc.vector.tensor_copy(HM[:, m, :, :], PS[:, 4 + m, :].rearrange("p (t n) -> p t n", t=2)
                                          ).then_inc(m_hm, 1)
                splits(c, 27, 29)

            def merge(i, first):
                c, g = C_MG + i * 12, G_MG + i * 4
                splits(c, 5, 7)
                if not first:
                    dve.wait_ge(mhi_ready, i)
                evacuate(c, 4, 1, SG[:, 0, :, :])
                scale(g + 1, SG[:, 0, :, :])
                if first:
                    ml_out(1, 0)
                splits(c, 7, 9)
                if first:
                    ml_out_lo(1, 0)
                    ml_out(1, 1)
                splits(c, 9, 11)
                if first:
                    ml_out_lo(1, 1)
                evacuate(c, 8, 0, SG[:, 1, :, :])
                scale(g + 2, SG[:, 1, :, :])
                splits(c, 11, 13)
                evacuate(c, 10, 1, T1[:, :, :])
                splits(c, 13, 15)
                evacuate(c, 12, 0, T2[:, :, :])
                splits(c, 15, 16)
                dve.wait_ge(sg_ready, i * 2 + 2)
                evacuated(g + 4)
                own.mark(tt(T1[:, :, :], T1[:, :, :], SG[:, 0, :, :], ALU.mult))
                own.mark(tt(T2[:, :, :], T2[:, :, :], SG[:, 1, :, :], ALU.mult))
                own.settle()
                tt(T1[:, :, :], T1[:, :, :], T2[:, :, :], ALU.add).then_inc(merged_ready, 1)
                dve.wait_ge(mhi_ready, i + 1)
                tt(MHL[:, bass.ds(i * 2, 2), S:2 * S], T1[:, :, :], MHL[:, bass.ds(i * 2, 2), 0:S].bitcast(F32),
                   ALU.subtract).then_inc(mlo_ready, 1)
                splits(c, 16, 17)

            merge(0, True)
            with dve.Fori(0, 7) as i:
                own.enter(i, 2)
                merge(i + 1, False)
                own.leave(7)

            def square(c0, g0, kts, n, name):
                per = len(kts)
                own.mark(nc.vector.memset(SQSUM[:, :, :], 0.0))
                own.settle()

                def body(i, final=False):
                    c = c0 + i * (2 * per)
                    for h in range(2):
                        end = (h + 1) * per
                        stop = end + (0 if final and h else 5)
                        splits(c, 5 + h * per, min(end + 3, stop), kts + kts)
                        evacuate(c, end, 1 - h, YC[:, 0:2, :])
                        evacuated(g0 + i * 2 + (h + 1))
                        xs = X[:, bass.ds(i * 4 + 2 * h, 2), :]
                        tt(xs, xs, YC[:, 0:2, :], ALU.add).then_inc(x_added, 1)
                        splits(c, min(end + 3, stop), min(end + 4, stop), kts + kts)
                        dve.wait_ge(x_squared, i * 2 + (4 + 8 * (n - 1) + h + 1))
                        dve.wait_ge(x_added, i * 2 + (8 * (n - 1) + h + 1))
                        tt(SQSUM[:, :, :], SQSUM[:, :, :], YC[:, 2:4, :], ALU.add).then_inc(sq_added, 1)
                        if name is not None:
                            for k in range(2):
                                gain_lo(name, n, i * 4 + (2 * h + k))
                        splits(c, min(end + 4, stop), stop, kts + kts)
                        dve.wait_ge(sq_added, i * 2 + (8 * (n - 1) + h + 1))

                last = name is None
                with dve.Fori(0, 3 if last else 4) as i:
                    body(i)
                if last:
                    body(3, True)

            def up(c0, g0, z0, ff, it0, n, cw):
                tiles = ff // P
                own.mark(nc.vector.memset(UP[:, :, :, 0:2], 0.0))
                own.settle()

                def taps(i, side, col, z):
                    dve.wait_ge(scaled, z)
                    for tap in (1, 0):
                        for m in range(2):
                            if tap == 1:
                                dve.wait_ge(tap_ready, i * 4 + (4 * it0 + 2 * side + m + 1))
                            else:
                                dve.wait_ge(conv_ready, i * 8 + (8 * it0 + 4 * side + m + 1))
                            stt(YC[:, 2 * side + m, :], UP[:, side, m, tap:tap + S],
                                VEC[:, bass.ds(col + (COL[cw] + 2 * tap * tiles + m), 1)], YC[:, 2 * side + m, :],
                                ALU.mult, ALU.add).then_inc(conv_ready, 1)

                def body(i, first):
                    c, g, z = c0 + i * 8, g0 + i * 2, z0 + i * 2
                    if first:
                        norm_rstd(n)
                    splits(c, 5, 7)
                    evacuate(c, 4, 1, UP[:, 0, :, 2:S + 2])
                    scale(g + 1, UP[:, 0, :, 2:S + 2])
                    splits(c, 7, 8)
                    taps(i, 0, i * 2, z + 1)
                    splits(c, 8, 11)
                    evacuate(c, 8, 0, UP[:, 1, :, 2:S + 2])
                    scale(g + 2, UP[:, 1, :, 2:S + 2])
                    splits(c, 11, 12)
                    taps(i, 1, i * 2 + tiles, z + 2)
                    dve.wait_ge(gate_act, i + (it0 + 1))
                    dve.wait_ge(conv_ready, i * 8 + (8 * it0 + 8))
                    tt(YC[:, 0:2, :], YC[:, 0:2, :], YC[:, 2:4, :], ALU.mult).then_inc(hid_ready, 1)
                    splits(c, 12, 13)
                    dve.wait_ge(hhi_ready, i + (it0 + 1))
                    tt(H[:, bass.ds(i * 2, 2), S:2 * S], YC[:, 0:2, :], H[:, bass.ds(i * 2, 2), 0:S].bitcast(F32),
                       ALU.subtract).then_inc(hlo_ready, 1)

                body(0, True)
                with dve.Fori(1, ff // GROUP) as i:
                    body(i, False)

            K4 = [4] * 4
            dve.wait_ge(vec_rest_landed, 16)
            square(C_OUT, G_OUT, K4, 1, "norm2_g")
            up(C_UP, G_UP, Z_UP, FF1, 0, 1, "conv_w")
            square(C_DN, G_DN, KT1, 2, "norm1_g_2")

            lam = VEC[:, COL["lru_lambda_2"]:COL["lru_lambda_2"] + 8]
            stt(C8W[:, 1, :], lam, -1.0, lam, ALU.mult, ALU.max).then_inc(c8_abs, 1)
            own.mark(nc.vector.tensor_scalar(C8W[:, 2, :], lam, -1.0, 0.0, ALU.mult, ALU.max))
            own.mark(nc.vector.memset(XL[:, :, 0:3], 0.0))
            own.settle()
            dve.wait_ge(c8_ln, 1)
            own.mark(tt(C8W[:, 2, :], C8W[:, 2, :], C8W[:, 0, :], ALU.add))
            own.settle()
            nc.vector.tensor_scalar(C8[:, :], C8W[:, 2, :], -LRU_C, None, ALU.mult).then_inc(c8_ready, 1)
            nc.vector.tensor_scalar(C8H[:, :], C8W[:, 2, :], -0.5 * LRU_C, None, ALU.mult).then_inc(c8_ready, 1)
            ba = COL["lru_ba_2"]
            nc.vector.tensor_scalar(HB[:, :], VEC[:, ba:ba + 16], 0.5, None, ALU.mult).then_inc(c8_ready, 1)

            norm_rstd(2)
            for n in range(4):
                splits(C_XL, 5 + 4 * n, 7 + 4 * n)
                evacuate(C_XL, 4 + 4 * n, 1 - n % 2, XL[:, 2 * n:2 * n + 2, 3:S + 3])
                scale(G_XL + n + 1, XL[:, 2 * n:2 * n + 2, 3:S + 3])
                splits(C_XL, 7 + 4 * n, 9 + 4 * n)

            for s in range(4):
                c, g = C_V + 4 * s, G_V + s
                splits(c, 5, 6)
                dve.wait_ge(scaled, Z_XL + s + 1)
                for tap in (2, 1, 0):
                    for m in range(2):
                        k = 2 * s + m
                        if tap == 2:
                            dve.wait_ge(xr_tap, k + 1)
                        else:
                            dve.wait_ge(xr_ready, 6 * s + 2 * (1 - tap) + m + 1)
                        stt(HL[:, k, :], XL[:, k, tap:tap + S], vec("lru_conv_w_2", 8 * tap + k), HL[:, k, :],
                            ALU.mult, ALU.add).then_inc(xr_ready, 1)
                splits(c, 6, 7)
                if s > 0:
                    dve.wait_ge(v_gelu, s)
                evacuate(c, 4, 1 - s % 2, ZT[:, :, :])
                scale(g + 1, ZT[:, :, :])
                splits(c, 7, 9)

            def normed_v(q):
                hs = slice(2 * q, 2 * q + 2)
                rows = [VGB[:, n, 256 * q:256 * q + 256].rearrange("p (h d) -> p h d", h=2) for n in range(2)]
                for b in range(2):
                    own.mark(stt(VTB[:, b, hs, :], VTB[:, b, hs, :], NMEAN[:, b:b + 1], rows[0], ALU.add, ALU.mult))
                own.settle()
                for b in range(2):
                    stt(VTB[:, b, hs, :], VTB[:, b, hs, :], VSQ[:, b:b + 1], rows[1], ALU.mult, ALU.add
                        ).then_inc(vn_ready, 1)

            def lru_parts(k):
                m = k % 2
                dve.wait_ge(lru_th, 3 * (k + 1))
                own.mark(stt(HL[:, k, :], RI[:, m, 1, :], 1.0, HL[:, k, :], ALU.add, ALU.mult))
                own.settle()
                stt(QQ[:, k, :], LA2[:, m, :], 1.0, LT[:, m, :], ALU.add, ALU.mult).then_inc(lru_q, 1)

            for s in range(4):
                c, g = C_U + 4 * s, G_U + s
                splits(c, 5, 6)
                splits(c, 6, 7)
                evacuate(c, 4, 1 - s % 2, GZ[:, 2 * s:2 * s + 2, :])
                scale(g + 1, GZ[:, 2 * s:2 * s + 2, :])
                if s == 1:
                    dve.wait_ge(ln_root, 1)
                    dve.wait_ge(vgb_landed, 16)
                    dve.wait_ge(ln_mean, 1)
                    own.mark(nc.vector.reciprocal(VSQ[:, :], VSQ[:, :]))
                    own.settle()
                if s > 0:
                    normed_v(s - 1)
                lru_parts(2 * s)
                splits(c, 7, 8)
                if s == 0:
                    dve.wait_ge(v_tokens, 8)
                    own.mark(nc.vector.tensor_reduce(NMEAN[:, :], VSUM[:, :, :], AX.X, ALU.add))
                    own.settle()
                    nc.vector.tensor_scalar(NMEAN[:, :], NMEAN[:, :], -1.0 / 1024, None, ALU.mult).then_inc(ln_mean, 1)
                lru_parts(2 * s + 1)
                splits(c, 8, 9)

            def scan(k):
                dve.wait_ge(lru_in, k // 4 + 1)
                nc.vector.tensor_tensor_scan(HL[:, k, :], AA[:, k, :], HL[:, k, :], 0.0, ALU.mult, ALU.add
                                             ).then_inc(lru_done, 1)

            def lru_input(n):
                dve.wait_ge(lru_mult, n + 1)
                tt(HL[:, 4 * n:4 * n + 4, :], HL[:, 4 * n:4 * n + 4, :], QQ[:, 4 * n:4 * n + 4, :], ALU.mult
                   ).then_inc(lru_in, 1)

            def gate_u(q):
                dve.wait_ge(u_gelu, 1)
                dve.wait_ge(mix_acc, q + 1)
                U = GZ[:, 2 * q:2 * q + 2, :]
                tt(U, U, PS[:, 7 - q % 2, :].rearrange("p (m n) -> p m n", m=2), ALU.mult).then_inc(mixed_ready, 1)

            def gate_lru(q):
                dve.wait_ge(g_gelu, q + 1)
                dve.wait_ge(lru_done, 2 * q + 2)
                tt(HL[:, 2 * q:2 * q + 2, :], HL[:, 2 * q:2 * q + 2, :], GL[:, 2 * q:2 * q + 2, :], ALU.mult
                   ).then_inc(lru_gated, 1)

            def out_scaled(q, name, row):
                src = GZ if q < 4 else HL
                dve.wait_ge(mixed_ready if q < 4 else lru_gated, 4)
                for k in (2 * q, 2 * q + 1):
                    stt(src[:, k % 8, :], src[:, k % 8, :], vec(name, k % 8), row, ALU.mult, ALU.mult
                        ).then_inc(out_gained, 1)

            def out_lo(q):
                dve.wait_ge(out_hi_ready, q + 1)
                src = GZ if q < 4 else HL
                tt(AHL[:, 2 * q:2 * q + 2, S:2 * S], src[:, 2 * (q % 4):2 * (q % 4) + 2, :],
                   AHL[:, 2 * q:2 * q + 2, 0:S].bitcast(F32), ALU.subtract).then_inc(out_lo_ready, 1)

            for s in range(4):
                c, g = C_GL + 4 * s, G_GL + s
                splits(c, 5, 6)
                if s == 0:
                    normed_v(3)
                    lru_input(0)
                if s == 1:
                    gate_u(0)
                    gate_u(1)
                    scan(2)
                    scan(3)
                if s == 3:
                    out_lo(1)
                    out_scaled(2, "gm_out_g_2", MU[:, :])
                splits(c, 6, 7)
                if s == 2:
                    dve.wait_ge(gm_root, 1)
                    own.mark(nc.vector.reciprocal(MU[:, :], MU[:, :]))
                    own.settle()
                evacuate(c, 4, 1 - s % 2, GL[:, 2 * s:2 * s + 2, :])
                scale(g + 1, GL[:, 2 * s:2 * s + 2, :])
                if s == 0:
                    lru_input(1)
                if s == 1:
                    gate_u(2)
                    gate_u(3)
                if s == 2:
                    out_scaled(0, "gm_out_g_2", MU[:, :])
                    gate_lru(2)
                if s == 3:
                    out_lo(2)
                    gate_lru(3)
                    out_scaled(3, "gm_out_g_2", MU[:, :])
                    out_lo(3)
                splits(c, 7, 8)
                if s == 0:
                    scan(0)
                    scan(1)
                if s == 1:
                    for k in range(4, 8):
                        scan(k)
                    gate_lru(0)
                    gate_lru(1)
                if s == 2:
                    out_lo(0)
                    out_scaled(1, "gm_out_g_2", MU[:, :])
                if s < 3:
                    splits(c, 8, 9)
            dve.wait_ge(lru_root, 1)
            own.mark(nc.vector.reciprocal(RSTD[:, :], RSTD[:, :]))
            own.settle()
            for q in range(4, 9):
                if q < 8:
                    out_scaled(q, "lru_out_g_2", RSTD[:, :])
                if q > 4:
                    out_lo(q - 1)
            splits(C_O2, 4, 5)

            square(C_O2, G_O2, K4, 3, "norm2_g_2")
            up(C_U2, G_U2, Z_U2, FF2, 22, 3, "ffn_conv_w_2")
            square(C_D2, G_D2, KT2, 4, None)
            for k in (14, 15):
                dve.wait_ge(x_squared, 4 + 8 * 4)
                own.mark(nc.vector.tensor_scalar(X[:, k, :], X[:, k, :], vec("final_g_2", k), None, ALU.mult))
            norm_rstd(4)
            dve.wait_ge(xg_ready, 14)
            own.settle()
            for q in range(4):
                xs = X[:, 4 * q:4 * q + 4, :]
                tt(xs, xs, RSTD[:, :].unsqueeze(1).to_broadcast([P, 4, S]), ALU.mult).then_inc(out_ready, 1)


_WEIGHTS = ["w_in", "w_proj_a", "w_proj_m", "w_out", "w_up", "w_down", "w_in_2", "w_out_2", "ffn_w_up_2",
            "ffn_w_down_2"]


def kernel(**inputs):
    import numpy as np
    import concourse.bacc as bacc
    from concourse.bass_utils import run_bass_kernel_spmd as run

    f = {n: np.asarray(a) for n, a in inputs.items()}
    arrays = {n: np.ascontiguousarray(f[n].reshape(f[n].shape[-2:])) for n in _WEIGHTS}
    arrays["x"] = np.ascontiguousarray(f["x"].reshape(S, KD, P).transpose(2, 1, 0))
    arrays["vec"] = np.ascontiguousarray(
        np.concatenate([f[name].reshape(tiles, P) for name, tiles in VECTORS]).T)
    w_in = arrays["w_in"]
    gate_columns = np.concatenate([w_in[:, OFF_FF:OFF_FF + FOX_HEADS], w_in[:, OFF_MF:OFF_MF + ML_HEADS],
                                   w_in[:, OFF_MI:OFF_MI + ML_HEADS]], axis=1)
    arrays["w_gate"] = np.ascontiguousarray(gate_columns.reshape(KD, P, 16).transpose(1, 0, 2))
    arrays["gate_b"] = np.concatenate([f["fox_f_bias"].reshape(1, -1), f["m_f_bias"].reshape(1, -1),
                                       f["m_i_bias"].reshape(1, -1)], axis=1).reshape(16, 1)
    arrays["gm_ws_2"] = np.ascontiguousarray(f["gm_ws_2"][0].transpose(2, 0, 1))
    arrays["gm_v_rows"] = np.concatenate([f["gm_v_g_2"].reshape(1, -1), f["gm_v_b_2"].reshape(1, -1)], axis=1)
    arrays["gm_bs_2"] = np.ascontiguousarray(f["gm_bs_2"].reshape(1, 8 * P))
    arrays["lru_wa_2"] = np.ascontiguousarray(f["lru_wa_2"][0].transpose(1, 0, 2))
    arrays["lru_wx_2"] = np.ascontiguousarray(f["lru_wx_2"][0].transpose(1, 0, 2))

    nc = bacc.Bacc("TRN2", target_bir_lowering=False, num_devices=1)
    w = {n: nc.dram_tensor(f"in_{n}", a.shape, F32, kind="ExternalInput").ap() for n, a in arrays.items()}
    w["out"] = nc.dram_tensor("out", (P, KD, S), F32, kind="ExternalOutput").ap()
    build(nc, w)
    r = run(nc, [{f"in_{n}": a for n, a in arrays.items()}], core_ids=[0])
    out = r.results[0]["out"]
    return np.ascontiguousarray(out.transpose(2, 1, 0)).reshape(1, S, D)
```
